# Optimizing a Trainium2 kernel written in Bass

```python
import jax, jax.numpy as jnp
from jax import lax
import numpy as np

D_MODEL = 2048
BATCH = 1
SEQ = 128
DEPTH = 1
DEC_BATCH = 1
DEC_SEQ = 128
PAST_LEN = 128

GRID_W = 64
NA_HEADS = 16
NA_HEAD_DIM = D_MODEL // NA_HEADS
NA_WIDTH = NA_HEADS * NA_HEAD_DIM
NA_WIN_ROWS = 8
NA_WIN_COLS = 16
Q_BLOCK = 128
SSD_D_INNER = 2 * D_MODEL
SSD_HEAD_DIM = 64
SSD_HEADS = SSD_D_INNER // SSD_HEAD_DIM
SSD_GROUPS = 8
SSD_STATE = 128
SSD_CONV = 5
SSD_CHUNK = 128
SSD_CONV_CH = SSD_D_INNER + 2 * SSD_GROUPS * SSD_STATE
PEER_HEADS = 8
PEER_KEY_DIM = 256
PEER_N_KEYS = 128
PEER_N_EXPERTS = PEER_N_KEYS * PEER_N_KEYS
PEER_TOPK = 16
PEER_TOKEN_BLOCK = 128
N_BRANCHES = 2
IN_SPLITS = (NA_WIDTH, 2 * NA_WIDTH, 3 * NA_WIDTH,
             3 * NA_WIDTH + SSD_D_INNER,
             3 * NA_WIDTH + SSD_D_INNER + SSD_CONV_CH,
             3 * NA_WIDTH + SSD_D_INNER + SSD_CONV_CH + 2 * SSD_HEADS)
IN_COLS = 3 * NA_WIDTH + SSD_D_INNER + SSD_CONV_CH + 2 * SSD_HEADS + N_BRANCHES * D_MODEL
RMS_EPS = 1e-6

kernel_name = "hybrid_na_ssd_peer_diffusion_step"

def rmsnorm(x, g):
    xf = x.astype(jnp.float32)
    y = xf * lax.rsqrt(jnp.mean(xf * xf, axis=-1, keepdims=True) + RMS_EPS)
    return (y * g.astype(jnp.float32)).astype(x.dtype)

def dwconv_centred(x, w, b):
    pad = SSD_CONV // 2
    y = lax.conv_general_dilated(x, w[:, None, :].astype(x.dtype), window_strides=(1,),
                                 padding=[(pad, pad)], dimension_numbers=('NWC', 'WIO', 'NWC'),
                                 feature_group_count=x.shape[-1])
    return y + b

def ssd_scan(x, dt, a, bm, cm, init):
    f32 = jnp.float32
    b, l, h, p = x.shape
    g, n = bm.shape[2], bm.shape[3]
    r = h // g
    nc = l // SSD_CHUNK
    xdt = (x.astype(f32) * dt[..., None]).reshape(b, nc, SSD_CHUNK, g, r, p)
    da = jnp.transpose((dt * a).reshape(b, nc, SSD_CHUNK, g, r), (0, 1, 3, 4, 2))
    acs = jnp.cumsum(da, axis=-1)
    bc = bm.astype(f32).reshape(b, nc, SSD_CHUNK, g, n)
    cc = cm.astype(f32).reshape(b, nc, SSD_CHUNK, g, n)
    lower = jnp.tril(jnp.ones((SSD_CHUNK, SSD_CHUNK), dtype=bool))
    seg = acs[..., :, None] - acs[..., None, :]
    lmat = jnp.where(lower, jnp.exp(jnp.where(lower, seg, 0.0)), 0.0)
    cb = jnp.einsum('bclgn,bcsgn->bcgls', cc, bc)
    y_diag = jnp.einsum('bcgls,bcgrls,bcsgrp->bclgrp', cb, lmat, xdt)
    decay = jnp.exp(acs[..., -1:] - acs)
    states = jnp.einsum('bcsgn,bcgrs,bcsgrp->bcgrpn', bc, decay, xdt)
    dtot = jnp.exp(acs[..., -1])

    def step(s, inp):
        st, d = inp
        return s * d[..., None, None] + st, s

    final, starts = lax.scan(step, init.astype(f32).reshape(b, g, r, p, n),
                             (jnp.moveaxis(states, 1, 0), jnp.moveaxis(dtot, 1, 0)))
    starts = jnp.moveaxis(starts, 0, 1)
    y_off = jnp.einsum('bclgn,bcgrpn,bcgrl->bclgrp', cc, starts, jnp.exp(acs))
    y = (y_diag + y_off).reshape(b, l, h, p)
    return y.astype(x.dtype), final.reshape(b, h, p, n).astype(init.dtype)

def ssd_branch(z, xbc, dt_raw, lp, init_f, init_b):
    b, l, _ = z.shape
    xbc = jax.nn.silu(dwconv_centred(xbc, lp['conv_w'], lp['conv_b']))
    xs, bm, cm = jnp.split(xbc, [SSD_D_INNER, SSD_D_INNER + SSD_GROUPS * SSD_STATE], axis=-1)
    xs = xs.reshape(b, l, SSD_HEADS, SSD_HEAD_DIM)
    bm = bm.reshape(b, l, SSD_GROUPS, SSD_STATE)
    cm = cm.reshape(b, l, SSD_GROUPS, SSD_STATE)
    dt = jax.nn.softplus(dt_raw.astype(jnp.float32).reshape(b, l, 2, SSD_HEADS)
                         + lp['ssd_dt_bias'].astype(jnp.float32))
    a = -jnp.exp(lp['ssd_a_log'].astype(jnp.float32))
    y_f, s_f = ssd_scan(xs, dt[:, :, 0], a[0], bm, cm, init_f)
    y_b, s_b = ssd_scan(xs[:, ::-1], dt[:, ::-1, 1], a[1], bm[:, ::-1], cm[:, ::-1], init_b)
    y = y_f + y_b[:, ::-1] + lp['ssd_d'][:, None] * xs
    y = y.reshape(b, l, SSD_D_INNER) * jax.nn.silu(z)
    yg = y.reshape(b, l, SSD_GROUPS, SSD_D_INNER // SSD_GROUPS).astype(jnp.float32)
    yg = yg * lax.rsqrt(jnp.mean(yg * yg, axis=-1, keepdims=True) + RMS_EPS)
    y = (yg.reshape(b, l, SSD_D_INNER) * lp['ssd_norm_g'].astype(jnp.float32)).astype(z.dtype)
    return y, s_f, s_b

def ctx_attention(q, k, v):
    b, s, h, dh = q.shape
    nb = s // Q_BLOCK
    qb = jnp.moveaxis(q.reshape(b, nb, Q_BLOCK, h, dh), 1, 0)
    scale = dh ** -0.5

    def block(qi):
        sc = jnp.einsum('bqhd,bkhd->bhqk', qi, k).astype(jnp.float32) * scale
        p = jax.nn.softmax(sc, axis=-1).astype(v.dtype)
        return jnp.einsum('bhqk,bkhd->bqhd', p, v)

    o = lax.map(block, qb)
    return jnp.moveaxis(o, 0, 1).reshape(b, s, h * dh)

def na_latent(q, k, v, k_ctx, v_ctx, rpb):
    b, t, h, dh = q.shape
    rows = t // GRID_W
    kr = min(NA_WIN_ROWS, rows)
    r = jnp.arange(rows)
    row_start = jnp.clip(r - kr // 2, 0, rows - kr)
    key_rows = row_start[:, None] + jnp.arange(kr)[None, :]
    col = jnp.arange(GRID_W)
    col_start = jnp.clip(col - NA_WIN_COLS // 2, 0, GRID_W - NA_WIN_COLS)
    col_ok = (col[None, :] >= col_start[:, None]) & (col[None, :] < col_start[:, None] + NA_WIN_COLS)
    n_win = kr * GRID_W
    mask = jnp.broadcast_to(col_ok[:, None, :], (GRID_W, kr, GRID_W)).reshape(GRID_W, n_win)
    qg = q.reshape(b, rows, GRID_W, h, dh)
    kg = k.reshape(b, rows, GRID_W, h, dh)[:, key_rows].reshape(b, rows, n_win, h, dh)
    vg = v.reshape(b, rows, GRID_W, h, dh)[:, key_rows].reshape(b, rows, n_win, h, dh)
    row_off = key_rows - r[:, None] + (NA_WIN_ROWS - 1)
    col_off = jnp.clip(col[None, :] - col[:, None], -(NA_WIN_COLS - 1), NA_WIN_COLS - 1) + (NA_WIN_COLS - 1)
    bias = rpb[:, row_off[:, None, :, None], col_off[None, :, None, :]]
    bias = bias.reshape(h, rows, GRID_W, n_win).astype(jnp.float32)
    scale = dh ** -0.5
    s_win = jnp.einsum('brqhd,brkhd->bhrqk', qg, kg).astype(jnp.float32) * scale + bias[None]
    s_win = jnp.where(mask, s_win, -jnp.inf)
    s_ctx = jnp.einsum('brqhd,bkhd->bhrqk', qg, k_ctx).astype(jnp.float32) * scale
    p = jax.nn.softmax(jnp.concatenate([s_win, s_ctx], axis=-1), axis=-1).astype(v.dtype)
    o = (jnp.einsum('bhrqk,brkhd->brqhd', p[..., :n_win], vg)
         + jnp.einsum('bhrqk,bkhd->brqhd', p[..., n_win:], v_ctx))
    return o.reshape(b, t, h * dh)

def peer(h, w_q, sub_keys, u, v):
    b, l, d = h.shape
    kk = PEER_TOPK
    q = (h @ w_q).reshape(b, l, PEER_HEADS, 2, PEER_KEY_DIM // 2)
    s = jnp.einsum('blhpk,hpnk->blhpn', q, sub_keys).astype(jnp.float32)
    sv, si = lax.top_k(s, kk)
    cand = sv[..., 0, :, None] + sv[..., 1, None, :]
    cv, ci = lax.top_k(cand.reshape(b, l, PEER_HEADS, kk * kk), kk)
    i1 = jnp.take_along_axis(si[..., 0, :], ci // kk, axis=-1)
    i2 = jnp.take_along_axis(si[..., 1, :], ci % kk, axis=-1)
    expert = i1 * PEER_N_KEYS + i2
    gate = jax.nn.softmax(cv, axis=-1).astype(h.dtype)
    t = b * l
    nb = t // PEER_TOKEN_BLOCK
    hb = h.reshape(nb, PEER_TOKEN_BLOCK, d)
    eb = expert.reshape(nb, PEER_TOKEN_BLOCK, PEER_HEADS * kk)
    gb = gate.reshape(nb, PEER_TOKEN_BLOCK, PEER_HEADS * kk)

    def block(args):
        hx, ex, gx = args
        act = jax.nn.gelu(jnp.einsum('tkd,td->tk', u[ex], hx), approximate=False)
        return jnp.einsum('tk,tkd->td', gx * act, v[ex])

    out = lax.map(block, (hb, eb, gb))
    return out.reshape(b, l, d)

def trunk_layer(x, lp, cvec, ctx_cache=None):
    b, l, _ = x.shape
    m = jnp.dot(jax.nn.silu(cvec), lp['ada_w']) + lp['ada_b']
    sh1, sc1, g1, sh2, sc2, g2 = [t[:, None, :] for t in jnp.split(m, 6, axis=-1)]
    h = rmsnorm(x, lp['norm1_g']) * (1 + sc1) + sh1
    q, k, v, z, xbc, dt_raw, gates = jnp.split(h @ lp['w_in'], IN_SPLITS, axis=-1)
    q = q.reshape(b, l, NA_HEADS, NA_HEAD_DIM)
    k = k.reshape(b, l, NA_HEADS, NA_HEAD_DIM)
    v = v.reshape(b, l, NA_HEADS, NA_HEAD_DIM)
    if ctx_cache is None:
        na = ctx_attention(q, k, v)
        init_f = jnp.zeros((b, SSD_HEADS, SSD_HEAD_DIM, SSD_STATE), x.dtype)
        init_b = init_f
    else:
        k_ctx, v_ctx, init_f, init_b = ctx_cache
        na = na_latent(q, k, v, k_ctx, v_ctx, lp['na_rpb'])
    ssd, s_f, s_b = ssd_branch(z, xbc, dt_raw, lp, init_f, init_b)
    g_na, g_ssd = jnp.split(jax.nn.sigmoid(gates), 2, axis=-1)
    mixed = (g_na * (na @ lp['w_na_proj']) + g_ssd * (ssd @ lp['w_ssd_proj'])) @ lp['w_out']
    x = x + g1 * mixed
    h2 = rmsnorm(x, lp['norm2_g']) * (1 + sc2) + sh2
    x = x + g2 * peer(h2, lp['peer_wq'], lp['peer_keys'], lp['peer_u'], lp['peer_v'])
    return x, (k, v, s_f, s_b)

def setup_inputs(seed: int = 0) -> dict:
    key = jax.random.key(seed)
    ks = jax.random.split(key, 32)
    nrm = lambda i, shape, s=1.0: jax.random.normal(ks[i], shape, jnp.float32) * s
    dt0 = jnp.exp(jax.random.uniform(ks[15], (DEPTH, 2, SSD_HEADS), jnp.float32,
                                     np.log(1e-3), np.log(1e-1)))
    return {
        'x_prompt': nrm(0, (BATCH, SEQ, D_MODEL)),
        'x_sample': nrm(1, (DEC_BATCH, DEC_SEQ, D_MODEL)),
        'c': nrm(2, (DEC_BATCH, D_MODEL)),
        'c_ctx': nrm(3, (D_MODEL,)),
        'cache_na_k': nrm(4, (DEC_BATCH, DEPTH, PAST_LEN, NA_HEADS, NA_HEAD_DIM)),
        'cache_na_v': nrm(5, (DEC_BATCH, DEPTH, PAST_LEN, NA_HEADS, NA_HEAD_DIM)),
        'state_ssd_fwd': nrm(6, (DEC_BATCH, DEPTH, SSD_HEADS, SSD_HEAD_DIM, SSD_STATE), 0.5),
        'state_ssd_bwd': nrm(7, (DEC_BATCH, DEPTH, SSD_HEADS, SSD_HEAD_DIM, SSD_STATE), 0.5),
        'ada_w': nrm(8, (DEPTH, D_MODEL, 6 * D_MODEL), 0.5 * D_MODEL ** -0.5),
        'ada_b': nrm(9, (DEPTH, 6 * D_MODEL), 0.02),
        'norm1_g': 1.0 + nrm(10, (DEPTH, D_MODEL), 0.02),
        'norm2_g': 1.0 + nrm(11, (DEPTH, D_MODEL), 0.02),
        'w_in': nrm(12, (DEPTH, D_MODEL, IN_COLS), D_MODEL ** -0.5),
        'conv_w': nrm(13, (DEPTH, SSD_CONV, SSD_CONV_CH), SSD_CONV ** -0.5),
        'conv_b': nrm(14, (DEPTH, SSD_CONV_CH), 0.02),
        'na_rpb': nrm(16, (DEPTH, NA_HEADS, 2 * NA_WIN_ROWS - 1, 2 * NA_WIN_COLS - 1), 0.5),
        'ssd_a_log': jnp.log(jax.random.uniform(ks[17], (DEPTH, 2, SSD_HEADS), jnp.float32, 1.0, 16.0)),
        'ssd_dt_bias': dt0 + jnp.log(-jnp.expm1(-dt0)),
        'ssd_d': 1.0 + nrm(18, (DEPTH, SSD_HEADS), 0.1),
        'ssd_norm_g': 1.0 + nrm(19, (DEPTH, SSD_D_INNER), 0.02),
        'w_na_proj': nrm(20, (DEPTH, NA_WIDTH, D_MODEL), NA_WIDTH ** -0.5),
        'w_ssd_proj': nrm(21, (DEPTH, SSD_D_INNER, D_MODEL), SSD_D_INNER ** -0.5),
        'w_out': nrm(22, (DEPTH, D_MODEL, D_MODEL), D_MODEL ** -0.5),
        'peer_wq': nrm(23, (DEPTH, D_MODEL, PEER_HEADS * PEER_KEY_DIM), D_MODEL ** -0.5),
        'peer_keys': nrm(24, (DEPTH, PEER_HEADS, 2, PEER_N_KEYS, PEER_KEY_DIM // 2), (PEER_KEY_DIM // 2) ** -0.5),
        'peer_u': nrm(25, (DEPTH, PEER_N_EXPERTS, D_MODEL), D_MODEL ** -0.5),
        'peer_v': nrm(26, (DEPTH, PEER_N_EXPERTS, D_MODEL)),
        'final_g': 1.0 + nrm(27, (D_MODEL,), 0.02),
    }

def reference(x_prompt, x_sample, c, c_ctx, cache_na_k, cache_na_v, state_ssd_fwd, state_ssd_bwd,
              ada_w, ada_b, norm1_g, norm2_g, w_in, conv_w, conv_b, na_rpb, ssd_a_log, ssd_dt_bias,
              ssd_d, ssd_norm_g, w_na_proj, w_ssd_proj, w_out, peer_wq, peer_keys, peer_u, peer_v,
              final_g):
    yp = x_prompt
    ys = x_sample
    new_k, new_v, new_f, new_b = [], [], [], []
    for i in range(DEPTH):
        lp = {'ada_w': ada_w[i], 'ada_b': ada_b[i], 'norm1_g': norm1_g[i], 'norm2_g': norm2_g[i],
              'w_in': w_in[i], 'conv_w': conv_w[i], 'conv_b': conv_b[i], 'na_rpb': na_rpb[i],
              'ssd_a_log': ssd_a_log[i], 'ssd_dt_bias': ssd_dt_bias[i], 'ssd_d': ssd_d[i],
              'ssd_norm_g': ssd_norm_g[i], 'w_na_proj': w_na_proj[i], 'w_ssd_proj': w_ssd_proj[i],
              'w_out': w_out[i], 'peer_wq': peer_wq[i], 'peer_keys': peer_keys[i],
              'peer_u': peer_u[i], 'peer_v': peer_v[i]}
        yp, (k_i, v_i, sf_i, sb_i) = trunk_layer(yp, lp, c_ctx[None, :])
        new_k.append(k_i)
        new_v.append(v_i)
        new_f.append(sf_i)
        new_b.append(sb_i)
        ys, _ = trunk_layer(ys, lp, c, (cache_na_k[:, i], cache_na_v[:, i],
                                        state_ssd_fwd[:, i], state_ssd_bwd[:, i]))
    y_prompt = rmsnorm(yp, final_g)
    y_sample = rmsnorm(ys, final_g)
    return (y_prompt, y_sample, jnp.stack(new_k, axis=1), jnp.stack(new_v, axis=1),
            jnp.stack(new_f, axis=1), jnp.stack(new_b, axis=1))


_drawn_inputs = setup_inputs


def setup_inputs(seed=0):
    import zlib

    import numpy as np

    out = dict(_drawn_inputs(seed))
    spreads = {}
    factors = {'na_rpb': 3.628,
     'ssd_d': 3.659,
     'ssd_norm_g': 15.752,
     'final_g': 7.901,
     'cache_na_k': 4.06,
     'cache_na_v': 3.459,
     'norm2_g': 3.282}
    for name, (base, spread) in spreads.items():
        noise = np.random.default_rng([zlib.crc32(name.encode()), seed]).standard_normal(out[name].shape)
        drawn = base * np.exp(spread * noise) if base else spread * noise
        out[name] = __import__('jax').numpy.asarray(drawn.astype(out[name].dtype))
    for name, factor in factors.items():
        out[name] = (out[name] * factor).astype(out[name].dtype)
    return out
```

```python
from contextlib import ExitStack

import concourse.bass as bass
from concourse import mybir

ALU = mybir.AluOpType
ACT = mybir.ActivationFunctionType
AX = mybir.AxisListType
F32 = mybir.dt.float32
F32R = mybir.dt.float32r
U32 = mybir.dt.uint32

P = 128
D = 2048
KT = D // P
NS = 2
T = NS * P
CH = 512
SLOTS = 4
HALVES = 2 * SLOTS
EPS = 1e-6
NA_HEADS = 16
GROUPS = 8
SSD_HEADS = 64
HPG = SSD_HEADS // GROUPS
HD = 64
D_IN = 2 * D
CONV_CH = D_IN + 2 * GROUPS * P
TAPS = 5
GRID_W = 64
WIN_COLS = 16
RPB_COLS = 2 * WIN_COLS - 1
RPB = 15 * RPB_COLS
PEER_HEADS = 8
TOPK = 16
SEL = PEER_HEADS * TOPK
UNROLL = 8
RING = 4
NEG = -1.0e30
LOWEST = -3.0e38

COL_Z = 3 * D
COL_XBC = COL_Z + D_IN
COL_DT = COL_XBC + CONV_CH
COL_GATES = COL_DT + 2 * SSD_HEADS

N_ADA, N_QK, N_V, N_Z, N_GATES, N_XBC, N_DT = 24, 8, 4, 8, 8, 12, 1
N_NAP, N_SSDP, N_OUT, N_WQ = 4, 8, 4, 4
C_ADA = 0
C_QK = C_ADA + N_ADA
C_V = C_QK + N_QK
C_Z = C_V + N_V
C_GATES = C_Z + N_Z
C_XBC = C_GATES + N_GATES
C_DT = C_XBC + N_XBC
C_NAP = C_DT + N_DT
C_SSDP = C_NAP + N_NAP
C_OUT = C_SSDP + N_SSDP
C_WQ = C_OUT + N_OUT
C_END = C_WQ + N_WQ

POOL_CONST = 41


def steps_of(eng, sem, before=0):
    count = [before, 0, 0]

    def mark(ins):
        count[0] += 1
        ins.then_inc(sem, 1)
        return count[0] + count[1]

    def link(ins):
        eng.wait_ge(sem, mark(ins))

    def enter(passed):
        count[1], count[2] = passed, count[0]

    def leave(passes, steps):
        assert count[0] - count[2] == steps, (count[0] - count[2], steps)
        count[0], count[1] = count[2] + passes * steps, 0

    return mark, link, enter, leave


def program(nc, a, o):
    ctx = ExitStack()
    with ctx:
        base = 16512

        def at(name, shape, dtype, kib):
            return nc.alloc_sbuf_tensor_at(name, shape, dtype, offset=base + int(kib * 1024))

        def sem(name):
            return ctx.enter_context(nc.semaphore(name))

        raw = at("raw", [P, SLOTS, 4, CH], F32, 0)
        w_lo = at("w_lo", [P, 2, 2, CH], F32R, 32)
        w_hi = at("w_hi", [P, 4, 2, CH], F32R, 191)
        h_hi = at("h_hi", [P, KT, T], F32R, 48)
        h_lo = at("h_lo", [P, KT, T], F32R, 64)
        qk_f = at("qk_f", [P, 2 * NA_HEADS, T], F32, 80)
        v_t = at("v_t", [P, NS, D], F32, 112)
        na_f = at("na_f", [P, KT, T], F32, 128)
        ident = at("ident", [P, P], F32, 144)
        up_eq = at("up_eq", [P, P], F32, 144.5)
        low_eq = at("low_eq", [P, P], F32, 145)
        low_st = at("low_st", [P, P], F32, 145.5)
        up_st = at("up_st", [P, P], F32, 146)
        window = at("window", [P, 2, GRID_W], F32, 146.5)
        par_f = at("par_f", [P, 4, P], F32, 147)
        mod_f = at("mod_f", [P, 96, NS], F32, 149)
        scale_f = at("scale_f", [P, 2, KT, NS], F32, 149.75)
        silu_c = at("silu_c", [P, NS, KT], F32, 150)
        c4 = at("c4", [P, KT, 4], F32R, 150.25)
        comb = at("comb", [4, NS], F32, 150.5)
        comb_b = at("comb_b", [5, NS, P], F32, 150.5625)
        small = at("small", [P, 64], F32, 151.5625)
        x_t = at("x_t", [P, NS, D], F32, 152)
        par_rows = at("par_rows", [P, 4, P], F32, 168)
        mod_tmp = at("mod_tmp", [P, 4, T], F32, 170)
        row = at("row", [4, 2, CH], F32, 174)
        bias_w = at("bias_w", [P, NA_HEADS, 2, GRID_W], F32, 152)
        kc_t = at("kc_t", [P, NA_HEADS, P], F32, 160)
        vc_t = at("vc_t", [P, NA_HEADS, P], F32, 168)
        q_s = at("q_s", [P, 2, T], F32, 176)
        k_s = at("k_s", [P, 2, P], F32, 178)
        kc_s = at("kc_s", [P, 2, P], F32, 179)
        v_s = at("v_s", [P, 2, 3, P], F32, 180)
        kc_f = at("kc_f", [P, 2, P], F32, 183)
        soft = at("soft", [P, 2, 3, P], F32, 184)
        stats = at("stats", [P, 2, 4], F32, 151.9375)
        soft_t = at("soft_t", [P, 2, 3, P], F32, 187)
        flip = at("flip", [P, P], F32, 188.5)
        k_t = at("k_t", [P, NA_HEADS, P], F32, 40)
        gate_buf = at("gate_buf", [P, 2, NS, CH], F32, 152)
        xs_t = at("xs_t", [P, GROUPS, NS, CH], F32, 80)
        b_f = at("b_f", [P, GROUPS, T], F32, 112)
        c_f = at("c_f", [P, GROUPS, T], F32, 120)
        b_t = at("b_t", [P, GROUPS, P], F32, 160)
        conv = at("conv", [P, 4, T], F32, 164)
        conv_s = at("conv_s", [P, 4, T], F32, 168)
        dt_w = at("dt_w", [P, NS, 2, SSD_HEADS], F32, 175.25)
        dt_l = at("dt_l", [P, NS, 2, SSD_HEADS], F32, 176.25)
        dt_par = at("dt_par", [P, 5, SSD_HEADS], F32, 172)
        dt_t = at("dt_t", [P, NS, 2, SSD_HEADS], F32, 173.25)
        da_t = at("da_t", [P, NS, 2, SSD_HEADS], F32, 174.25)
        m_s = at("m_s", [P, NS, 2, HPG, P], F32, 48)
        decay_s = at("decay_s", [P, NS, HPG, P], F32, 64)
        mix_s = at("mix_s", [P, 2, HPG, P], F32, 72)
        xdt = at("xdt", [P, 2, CH], F32, 152)
        cbm = at("cbm", [P, 2, P], F32, 156)
        bc_s = at("bc_s", [P, 2, T], F32, 157)
        c_y = at("c_y", [P, P], F32, 159)
        xdec = at("xdec", [P, 2, CH], F32, 164)
        y_w = at("y_w", [P, NS, CH], F32, 168)
        y_n = at("y_n", [P, NS, CH], F32, 176.25)
        y_t = at("y_t", [P, CH], F32, 188.25)
        st_out = at("st_out", [P, 2, 4, P], F32, 180.25)
        s0_raw = at("s0_raw", [P, 2, 4, P], F32, 184.25)
        e_acs = at("e_acs", [P, 4, SSD_HEADS], F32, 175.25)
        z_g = at("z_g", [P, NS, CH], F32, 40)
        s0_t = at("s0_t", [P, 2, CH], F32, 44)
        y_f = at("y_f", [P, 2 * KT, T], F32, 80)
        junk = at("junk", [P, NS * D], F32, 80)
        na_hi = at("na_hi", [P, KT, T], F32R, 112)
        na_lo = at("na_lo", [P, KT, T], F32R, 48)
        y_hi = at("y_hi", [P, 2 * KT, T], F32R, 112)
        y_lo = at("y_lo", [P, 2 * KT, T], F32R, 152)
        gate_g = at("gate_g", [P, 2, 4, T], F32, 40)
        gated = at("gated", [P, 4, T], F32, 184)
        mix_f = at("mix_f", [P, KT, T], F32, 64)
        mix_lo = at("mix_lo", [P, KT, T], F32R, 64)
        mix_hi = at("mix_hi", [P, KT, T], F32R, 48)
        x2_t = at("x2_t", [P, NS, D], F32, 80)
        g_rows = at("g_rows", [5, 2, D], F32, 96)
        g1_b = at("g1_b", [P, 2, NS, CH], F32, 152)
        res = at("res", [P, NS, CH], F32, 184)
        xn2_t = at("xn2_t", [P, NS, D], F32, 112)
        h2_t = at("h2_t", [P, NS, D], F32, 128)
        keys_r = at("keys_r", [P, 2 * PEER_HEADS, P], F32, 176)
        keys_t = at("keys_t", [P, 2 * PEER_HEADS, P], F32, 168)
        peer_q = at("peer_q", [P, 2 * PEER_HEADS, T], F32, 152)
        score = at("score", [P, NS, 2 * PEER_HEADS, P], F32, 112)
        top_v = at("top_v", [P, 2 * PEER_HEADS, TOPK], F32, 184)
        top_i = at("top_i", [P, 2 * PEER_HEADS, TOPK], U32, 185)
        top_f = at("top_f", [P, 2 * PEER_HEADS, TOPK], F32, 186)
        cand = at("cand", [P, PEER_HEADS, TOPK * TOPK], F32, 152)
        cand_v = at("cand_v", [P, PEER_HEADS, TOPK], F32, 187)
        cand_i = at("cand_i", [P, PEER_HEADS, TOPK], U32, 187.5)
        part_i = at("part_i", [P, 2, SEL], U32, 188)
        part_f = at("part_f", [P, 2, SEL], F32, 189)
        key_f = at("key_f", [P, 2, SEL], F32, 190)
        hot = at("hot", [P, SEL, TOPK], F32, 160)
        expert = at("expert", [P, NS, SEL], U32, 168)
        gate_t = at("gate_t", [P, NS, SEL], F32, 169)
        gate_sum = at("gate_sum", [P, PEER_HEADS], F32, 170)
        u_r = at("u_r", [P, RING, D], F32, 0)
        v_r = at("v_r", [P, RING, D], F32, 32)
        peer_t = at("peer_t", [P, NS, D], F32, 64)
        index_c = at("index_c", [P, RING], U32, 171)
        gate_c = at("gate_c", [P, RING], F32, 171.25)
        act_c = at("act_c", [P, RING], F32, 171.5)
        gelu_c = at("gelu_c", [P, RING], F32, 171.75)
        coef_c = at("coef_c", [P, RING], F32, 172)
        final_b = at("final_b", [P, D], F32, 176)

        psum = [ctx.enter_context(nc.psum_tensor(f"bank{n}", [P, 512], F32)) for n in range(8)]
        acc = [[psum[0], psum[1]], [psum[2], psum[3]]]

        mod_rows = nc.dram_tensor("mod_rows", (4, 6 * D), F32, kind="Internal").ap()
        z_rows = nc.dram_tensor("z_rows", (P, NS, D_IN), F32, kind="Internal").ap()
        gate_rows = nc.dram_tensor("gate_rows", (P, 2 * KT, T), F32, kind="Internal").ap()

        raw_full = [sem(f"raw_full{n}") for n in range(SLOTS)]
        hi_done = sem("hi_done")
        lo_done = sem("lo_done")
        split_used = sem("split_used")
        evac_a = sem("evac_a")
        evac_v = sem("evac_v")
        pool_const = sem("pool_const")
        par_in = sem("par_in")
        x_in = sem("x_in")
        par_t = sem("par_t")
        par_done = sem("par_done")
        c_silu = sem("c_silu")
        c_ready = sem("c_ready")
        row_used = sem("row_used")
        row_saved = [sem(f"row_saved{n}") for n in range(2)]
        mod_ready = sem("mod_ready")
        sumsq = sem("sumsq")
        rms_done = sem("rms_done")
        xn_ready = sem("xn_ready")
        nt_full = sem("nt_full")
        nt_mod = sem("nt_mod")
        nt_hi = sem("nt_hi")
        nt_lo = sem("nt_lo")
        cache_in = sem("cache_in")
        bias_turn = sem("bias_turn")
        bias_done = sem("bias_done")
        att_stage = sem("att_stage")
        att_kt = sem("att_kt")
        att_kc = sem("att_kc")
        att_s = sem("att_s")
        att_m = sem("att_m")
        att_e = sem("att_e")
        att_p = sem("att_p")
        att_pt = sem("att_pt")
        att_pc = sem("att_pc")
        att_o = sem("att_o")
        att_oc = sem("att_oc")
        kv_out = sem("kv_out")
        gate_saved = [sem(f"gate_saved{n}") for n in range(2)]
        conv_done = sem("conv_done")
        conv_silu = sem("conv_silu")
        conv_turn = sem("conv_turn")
        turn_copied = sem("turn_copied")
        dt_exp = sem("dt_exp")
        dt_ready = sem("dt_ready")
        z_in = [sem(f"z_in{s}") for s in range(NS)]
        s0_in = sem("s0_in")
        ssd_acs = sem("ssd_acs")
        ssd_e = sem("ssd_e")
        ssd_stage = sem("ssd_stage")
        ssd_cb = sem("ssd_cb")
        ssd_seg = sem("ssd_seg")
        ssd_y = sem("ssd_y")
        ssd_aux = sem("ssd_aux")
        ssd_s0 = sem("ssd_s0")
        ssd_yt = sem("ssd_yt")
        ssd_exp = sem("ssd_exp")
        ssd_s0c = sem("ssd_s0c")
        ssd_stc = sem("ssd_stc")
        st_saved = sem("st_saved")
        ssd_rms = sem("ssd_rms")
        ssd_yn = sem("ssd_yn")
        ssd_ytc = sem("ssd_ytc")
        ssd_cbm = sem("ssd_cbm")
        ssd_mix = sem("ssd_mix")
        ssd_yw = sem("ssd_yw")
        na_split = sem("na_split")
        na_ready = sem("na_ready")
        y_split = sem("y_split")
        y_ready = sem("y_ready")
        gate_in = [sem(f"gate_in{p}") for p in range(2)]
        mix_sum = sem("mix_sum")
        mix_split = sem("mix_split")
        mix_ready = sem("mix_ready")
        x2_in = sem("x2_in")
        g1_bc = sem("g1_bc")
        x2_ready = sem("x2_ready")
        h2_turn = sem("h2_turn")
        h2_copied = sem("h2_copied")
        keys_in = sem("keys_in")
        keys_turn = sem("keys_turn")
        keys_ready = sem("keys_ready")
        score_done = sem("score_done")
        score_in = sem("score_in")
        gate_max = sem("gate_max")
        gate_exp = sem("gate_exp")
        chosen = sem("chosen")
        staged = sem("staged")
        u_in = [sem(f"u_in{n}") for n in range(RING)]
        v_in = [sem(f"v_in{n}") for n in range(RING)]
        u_used = sem("u_used")
        v_used = sem("v_used")
        gelu_done = sem("gelu_done")
        coef_ready = sem("coef_ready")
        g2_bc = sem("g2_bc")
        final_in = sem("final_in")
        x3_ready = sem("x3_ready")
        x3_rms = sem("x3_rms")
        out_ready = sem("out_ready")
        out_saved = sem("out_saved")
        dve_chain = sem("dve_chain")
        act_chain = sem("act_chain")

        block = ctx.enter_context(nc.Block())

        @block.sync
        def _(sp):
            for s, name in enumerate(("x_prompt", "x_sample")):
                sp.dma_start(x_t[:, s, :], a[name][0]).then_inc(x_in, 16)

            def load(w, c, row0, col, width=CH, first=False):
                for s in range(SLOTS):
                    if not first:
                        split = c * HALVES - HALVES + 2 * s + 2
                        sp.wait_ge(hi_done, split)
                        sp.wait_ge(lo_done, split)
                    rows = w[row0 + s * 512:row0 + (s + 1) * 512, col]
                    sp.dma_start(raw[:, s, :, 0:width], rows.rearrange("(k p) n -> p k n", p=P)) \
                        .then_inc(raw_full[s], 16)

            def section(w, c0, n, col0, row0=0):
                with sp.Fori(0, n) as j:
                    load(w, c0 + j, row0, bass.ds(col0 + j * CH, CH))

            ada, w_in = a["ada_w"][0], a["w_in"][0]
            load(ada, C_ADA, 0, slice(0, CH), first=True)
            with sp.Fori(1, N_ADA) as j:
                load(ada, C_ADA + j, 0, bass.ds(j * CH, CH))
            section(w_in, C_QK, N_QK + N_V, 0)
            section(w_in, C_Z, N_Z, COL_Z)
            section(w_in, C_GATES, N_GATES, COL_GATES)
            sp.wait_ge(evac_a, C_Z)
            sp.dma_start(o["new_na_v"][0, 0].rearrange("t h d -> t (h d)"), v_t[:, 0, :]).then_inc(kv_out, 16)
            sp.wait_ge(att_kc, 2 * NA_HEADS)
            sp.dma_start(o["new_na_k"][0, 0], k_t[:]).then_inc(kv_out, 16)
            section(w_in, C_XBC, N_XBC, COL_XBC)
            load(w_in, C_DT, 0, slice(COL_DT, COL_DT + P), width=P)
            sp.wait_ge(kv_out, 32)

            load(a["w_na_proj"][0], C_NAP, 0, slice(0, CH))
            for p in range(2):
                sp.wait_ge(gate_saved[p], 8 * (N_Z + N_GATES))
            states = [a[f"state_ssd_{d}"][0, 0].rearrange("h p n -> (h p) n").rearrange("(g b r) n -> r g b n", b=4, r=P)
                      for d in ("fwd", "bwd")]

            def ssd_load(g, first=False):
                for s in range(NS):
                    if not first:
                        sp.wait_ge(ssd_yw, 2 * g - 1 + s)
                    sp.dma_start(z_g[:, s, :], z_rows[:, s, bass.ds(g * CH, CH)]).then_inc(z_in[s], 16)
                if not first:
                    sp.wait_ge(ssd_s0, g)
                for d in range(2):
                    sp.dma_start(s0_raw[:, d], states[d][:, bass.ds(g, 1)].rearrange("r g b n -> r (g b) n")) \
                        .then_inc(s0_in, 16)
            ssd_load(0, first=True)
            with sp.Fori(1, GROUPS) as g:
                ssd_load(g)
            sp.wait_ge(st_saved, 32 * GROUPS)

            w_na, w_ssd = a["w_na_proj"][0], a["w_ssd_proj"][0]
            with sp.Fori(1, N_NAP) as j:
                load(w_na, C_NAP + j, 0, bass.ds(j * CH, CH))
            for j in range(N_SSDP // 2):
                for half in range(2):
                    load(w_ssd, C_SSDP + 2 * j + half, (1 - half) * D, slice(j * CH, (j + 1) * CH))
            section(a["w_out"][0], C_OUT, N_OUT, 0)
            section(a["peer_wq"][0], C_WQ, N_WQ, 0)

            for s, name in enumerate(("y_prompt", "y_sample")):
                sp.wait_ge(out_ready, s + 1)
                sp.dma_start(o[name][0], peer_t[:, s, :]).then_inc(out_saved, 16)
            sp.wait_ge(out_saved, 32)
            for n in range(2):
                sp.wait_ge(row_saved[n], 8 * N_ADA)

        @block.gpsimd
        def _(pool):
            for t, value in ((ident, 0.0), (up_eq, 1.0), (low_eq, 1.0), (low_st, 1.0), (up_st, 1.0),
                             (window, 0.0), (comb, 0.0), (comb_b, 0.0), (flip, 0.0)):
                pool.memset(t[:], value).then_inc(pool_const, 1)
            rows = lambda x: x.rearrange("(r p) -> r p", p=P)
            taps = [rows(a["conv_w"][0, t]) for t in range(TAPS)]
            nb = CONV_CH // P
            for n, p0, x in ((0, 0, rows(a["ada_b"][0])), (0, 96, rows(a["norm1_g"][0])),
                             (0, 112, rows(a["norm2_g"][0])),
                             (1, 0, taps[0]), (1, nb, taps[1]), (1, 2 * nb, rows(a["ssd_norm_g"][0])),
                             (2, 0, taps[2]), (2, nb, taps[3]), (2, 96, rows(a["c_ctx"])),
                             (2, 112, rows(a["c"][0])),
                             (3, 0, taps[4]), (3, nb, rows(a["conv_b"][0]))):
                pool.dma_start(par_rows[p0:p0 + x.shape[0], n, :], x).then_inc(par_in, 16)
            for n in range(TOPK):
                pool.memset(small[:, 32 + n:33 + n], float(n)).then_inc(pool_const, 1)
            _, link, _, _ = steps_of(pool, pool_const, before=9 + TOPK)
            pool.wait_ge(pool_const, 9 + TOPK)

            def select(out, pattern, op, fill, start, step):
                link(pool.affine_select(out=out, in_=out, pattern=pattern, compare_op=op, fill=fill,
                                              base=start, channel_multiplier=step))

            select(ident[:], [[-1, P]], ALU.not_equal, 1.0, 0, 1)
            select(up_eq[:], [[1, P]], ALU.is_ge, 0.0, 0, -1)
            select(low_eq[:], [[-1, P]], ALU.is_ge, 0.0, 0, 1)
            select(low_st[:], [[-1, P]], ALU.is_gt, 0.0, 0, 1)
            select(up_st[:], [[1, P]], ALU.is_gt, 0.0, 0, -1)
            edge = GRID_W - WIN_COLS
            for half in range(2):
                w = window[half * GRID_W:(half + 1) * GRID_W]
                select(w[:, :, 0:edge], [[0, 2], [1, edge]], ALU.is_ge, NEG, WIN_COLS // 2, -1)
                select(w[:, :, WIN_COLS:], [[0, 2], [-1, edge]], ALU.is_ge, NEG, WIN_COLS // 2 - 1 - WIN_COLS, 1)
            for n in range(2):
                select(comb[:], [[-1, NS]], ALU.not_equal, 1.0, -2 * n, 1)
            for n in range(3):
                select(comb_b[:], [[-1 if n < 2 else 0, NS], [0, P]], ALU.not_equal, 1.0, -2 * n, 1)
            for half in range(2):
                part = slice(half * GRID_W, (half + 1) * GRID_W)
                select(flip[part, part], [[1, GRID_W]], ALU.not_equal, 1.0, 1 - GRID_W, 1)

            pool.wait_ge(nt_lo, 4)
            for n in range(2):
                pool.wait_ge(row_saved[n], 8 * N_ADA)
            pool.dma_start(kc_t[:], a["cache_na_k"][0, 0]).then_inc(cache_in, 16)
            pool.dma_start(vc_t[:], a["cache_na_v"][0, 0]).then_inc(cache_in, 16)
            rpb = a["na_rpb"]
            for r in range(2):
                for kr in range(2):
                    strip = bass.AP(rpb.tensor, (7 + kr - r) * RPB_COLS + WIN_COLS - GRID_W,
                                    [[1, GRID_W], [RPB, NA_HEADS], [1, GRID_W]])
                    pool.dma_start(bias_w[r * GRID_W:(r + 1) * GRID_W, :, kr, :], strip).then_inc(cache_in, 16)
            pool.wait_ge(evac_a, C_Z)
            pool.wait_ge(evac_v, C_Z)

            def stage(h, p, first=False):
                if not first:
                    pool.wait_ge(att_s, h - 1)
                    pool.wait_ge(att_o, h - 1)
                for dst, src in ((q_s[:, p, :], qk_f[:, bass.ds(h, 1), :]),
                                 (k_s[:, p, :], qk_f[:, bass.ds(NA_HEADS + h, 1), 0:P]),
                                 (kc_s[:, p, :], kc_t[:, bass.ds(h, 1), :]),
                                 (v_s[:, p, 0, :], v_t[:, 0, bass.ds(h * P, P)]),
                                 (v_s[:, p, 1, :], v_t[:, 1, bass.ds(h * P, P)]),
                                 (v_s[:, p, 2, :], vc_t[:, bass.ds(h, 1), :])):
                    pool.tensor_copy(dst, src if len(src.shape) == 2 else src.rearrange("p a b -> p (a b)")) \
                        .then_inc(att_stage, 1)
            for p in range(2):
                stage(p, p, first=True)
            with pool.Fori(1, NA_HEADS // 2) as i:
                for p in range(2):
                    stage(2 * i + p, p)

            pool.wait_ge(att_stage, 6 * NA_HEADS)
            for n, x in enumerate((a["ssd_dt_bias"][0, 0], a["ssd_dt_bias"][0, 1], a["ssd_a_log"][0, 0],
                                   a["ssd_a_log"][0, 1], a["ssd_d"][0])):
                pool.dma_start(dt_par[:, n, :], x.partition_broadcast(P)).then_inc(cache_in, 16)

            pool.wait_ge(dt_ready, 3)

            def ssd_group(g, first=False):
                if not first:
                    pool.wait_ge(ssd_cb, 2 * g)
                for n, x in enumerate((b_f, c_f)):
                    pool.tensor_copy(bc_s[:, n, :], x[:, bass.ds(g, 1), :].rearrange("p a t -> p (a t)")) \
                        .then_inc(ssd_stage, 1)
                for s in range(NS):
                    if not first:
                        pool.wait_ge(ssd_seg, 2 * g - 1 + s)
                    for d, mask in enumerate((low_st, up_st)):
                        pool.tensor_tensor(m_s[:, s, d], mask[:].unsqueeze(1).broadcast_to([P, HPG, P]),
                                           da_t[:, s, d, bass.ds(g * HPG, HPG)].unsqueeze(2).broadcast_to([P, HPG, P]),
                                           ALU.mult).then_inc(ssd_stage, 1)
                if not first:
                    pool.wait_ge(ssd_aux, 2 * g)
                pool.tensor_copy(c_y[:], c_f[:, bass.ds(g, 1), P:T].rearrange("p a t -> p (a t)")) \
                    .then_inc(ssd_stage, 1)
            pool.wait_ge(conv_silu, N_XBC)
            for p in range(2):
                pool.wait_ge(gate_saved[p], 8 * (N_Z + N_GATES))
            ssd_group(0, first=True)
            with pool.Fori(1, GROUPS) as g:
                ssd_group(g)

            pool.wait_ge(ssd_yw, 2 * GROUPS)
            pool.wait_ge(ssd_aux, 2 * GROUPS)

            def load_gates(n):
                pool.dma_start(gate_g[:, n % 2], gate_rows[:, 4 * n:4 * n + 4, :]).then_inc(gate_in[n % 2], 16)
            for n in range(2):
                load_gates(n)
            for n in range(2, 6):
                pool.wait_ge(evac_v, C_NAP + n - 2 + 1)
                load_gates(n)
            pool.wait_ge(y_ready, 2)
            for s, name in enumerate(("x_prompt", "x_sample")):
                pool.dma_start(x2_t[:, s, :], a[name][0]).then_inc(x2_in, 16)
            for n, col in enumerate((2 * D, 5 * D)):
                pool.dma_start(g_rows[0:4, n, :], mod_rows[:, col:col + D]).then_inc(x2_in, 16)
                pool.dma_start(g_rows[4:5, n, :], a["ada_b"][:, col:col + D]).then_inc(x2_in, 16)
            for n in range(6, 8):
                pool.wait_ge(evac_v, C_SSDP + 2 * (n - 6) + 2)
                load_gates(n)
            pool.wait_ge(split_used, C_OUT * HALVES)
            pool.dma_start(keys_r[:], a["peer_keys"][0].rearrange("h q n k -> n (h q) k")).then_inc(keys_in, 16)
            pool.wait_ge(keys_turn, 1)
            pool.dma_start(final_b[:], a["final_g"].partition_broadcast(P)).then_inc(final_in, 16)

            pool.wait_ge(split_used, C_END * HALVES)
            u_rows, v_rows = a["peer_u"][0], a["peer_v"][0]

            def gather(e, s, n, col, first=False):
                if not first:
                    pool.wait_ge(u_used, e - RING + 1)
                    pool.wait_ge(v_used, e - RING + 2 + s)
                    pool.wait_ge(pool_const, POOL_CONST)
                pool.tensor_copy(index_c[:, n:n + 1], expert[:, s, bass.ds(col, 1)]).then_inc(staged, 1)
                pool.wait_ge(staged, 2 * e + 1)
                pool.tensor_copy(gate_c[:, n:n + 1], gate_t[:, s, bass.ds(col, 1)]).then_inc(staged, 1)
                for rows, ring, landed in ((u_rows, u_r, u_in), (v_rows, v_r, v_in)):
                    pool.indirect_dma_start(ring[:, n], None, rows, bass.IndirectOffsetOnAxis(
                        ap=index_c[:, n:n + 1], axis=0)).then_inc(landed[n], 16)

            for s in range(NS):
                pool.wait_ge(chosen, s + 1)
                if s == 0:
                    for n in range(UNROLL):
                        gather(n, 0, n % RING, n, first=n < RING)
                with pool.Fori(1 - s, SEL // UNROLL) as i:
                    for n in range(UNROLL):
                        gather(s * SEL + UNROLL * i + n, s, n % RING, UNROLL * i + n)

        @block.scalar
        def _(act):
            _, link, _, _ = steps_of(act, act_chain)

            def split(c, h, first=False):
                g = c * HALVES + h
                if h % 2 == 0:
                    act.wait_ge(raw_full[h // 2], 16 * c + 16)
                if not first:
                    act.wait_ge(split_used, g - 3)
                act.activation(w_hi[:, h % 4], raw[:, h // 2, 2 * (h % 2):2 * (h % 2) + 2, :], ACT.Copy) \
                    .then_inc(hi_done, 1)

            def unit(c, evacuate, late=None, late_at=6, last=False):
                for h in range(2, HALVES):
                    split(c, h, first=isinstance(c, int) and c == 0 and h < 4)
                    if h == late_at and late is not None:
                        late()
                if not last:
                    split(c + 1, 0)
                    split(c + 1, 1)
                act.wait_ge(split_used, c * HALVES + HALVES)
                evacuate()

            def section(c0, n, evacuate, peeled=0, late=None):
                for j in range(2 * peeled):
                    unit(c0 + j, lambda: evacuate(j, (c0 + j) % 2), (lambda: late(j - 1)) if late and j else None)
                with act.Fori(peeled, n // 2) as i:
                    for p in range(2):
                        j = 2 * i + p
                        unit(c0 + j, lambda: evacuate(j, (c0 + p) % 2), (lambda: late(j - 1)) if late else None)

            act.wait_ge(x_in, 32)
            for s in range(NS):
                act.activation(junk[:, s * D:(s + 1) * D], x_t[:, s, :], ACT.Square, accum_out=small[:, s:s + 1]) \
                    .then_inc(sumsq, 1)
            act.wait_ge(sumsq, NS)
            act.activation(small[:, 2:4], small[:, 0:2], ACT.Sqrt, bias=EPS, scale=1.0 / D).then_inc(rms_done, 1)
            act.wait_ge(par_done, 3)
            link(act.activation(silu_c[:], par_f[:, 2, 96:P].rearrange("p (s k) -> p s k", s=NS), ACT.Silu))
            act.activation(c4[:, :, 0:2], silu_c[:].rearrange("p s k -> p k s"), ACT.Copy).then_inc(c_silu, 1)

            for h in range(2):
                split(C_ADA, h, first=True)

            def ada(j, par):
                if not isinstance(j, int):
                    act.wait_ge(row_used, j - 1)
                    act.wait_ge(row_saved[par], 8 * (j - par))
                act.activation(row[:, par, :], acc[par][0][0:4, :], ACT.Copy).then_inc(evac_a, 1)
                act.wait_ge(evac_a, j + 1)
                act.dma_start(mod_rows[:, bass.ds(j * CH, CH)], row[:, par, :]).then_inc(row_saved[par], 16)
            section(C_ADA, N_ADA, ada, peeled=1)

            for q in range(4):
                act.wait_ge(nt_mod, 8 * q + 8)
                act.activation(h_hi[:, 4 * q:4 * q + 4, :], mod_tmp[:], ACT.Copy).then_inc(nt_hi, 1)

            def qk(j, par):
                act.activation(qk_f[:, bass.ds(4 * j, 2), :], acc[par][0][:].rearrange("p (b t) -> p b t", b=2),
                               ACT.Copy).then_inc(evac_a, 1)
            section(C_QK, N_QK, qk)

            def v(j, par):
                act.activation(v_t[:, 0, bass.ds(j * CH, CH)], acc[par][0][:], ACT.Copy).then_inc(evac_a, 1)
            section(C_V, N_V, v)

            def keys(h, p):
                act.wait_ge(att_kt, h + 1)
                if not isinstance(h, int):
                    act.wait_ge(att_s, h - 1)
                act.activation(kc_f[:, p, :], psum[p][:, P:2 * P], ACT.Copy).then_inc(att_kc, 1)
                act.activation(k_t[:, bass.ds(h, 1), :].rearrange("p a d -> p (a d)"), psum[p][:, 0:P], ACT.Copy) \
                    .then_inc(att_kc, 1)

            def exponentials(h, p):
                act.wait_ge(att_m, 4 * h + 4)
                act.activation(soft[:, p, 0], soft[:, p, 0], ACT.Exp, bias=stats[:, p, 0:1],
                               accum_out=stats[:, p, 2:3]).then_inc(att_e, 1)
                act.activation(soft[:, p, 1:3], soft[:, p, 1:3], ACT.Exp, bias=stats[:, p, 1:2],
                               accum_out=stats[:, p, 3:4]).then_inc(att_e, 1)

            def turned(h, p, first=False):
                act.wait_ge(att_pt, h + 1)
                if not first:
                    act.wait_ge(att_o, h - 1)
                act.activation(soft_t[:, p], psum[6 + p][:, 0:3 * P].rearrange("p (a b) -> p a b", a=3), ACT.Copy) \
                    .then_inc(att_pc, 1)

            keys(0, 0)
            exponentials(0, 0)
            keys(1, 1)
            turned(0, 0, first=True)
            exponentials(1, 1)
            with act.Fori(1, NA_HEADS // 2) as i:
                for p in range(2):
                    h = 2 * i + p
                    keys(h, p)
                    turned(h - 1, 1 - p, first=False)
                    exponentials(h, p)
            turned(NA_HEADS - 1, 1)

            def gates(c0, func, rows, saved):
                def evacuate(j, par):
                    if not isinstance(j, int):
                        act.wait_ge(gate_saved[par], saved + 8 * (j - par))
                    elif saved:
                        act.wait_ge(gate_saved[par], saved)
                    act.activation(gate_buf[:, par, 0, :], acc[par][0][:], func)
                    act.activation(gate_buf[:, par, 1, :], acc[par][1][:], func).then_inc(evac_a, 1)
                    act.wait_ge(evac_a, c0 + j + 1)
                    act.dma_start(rows(j), gate_buf[:, par]).then_inc(gate_saved[par], 16)
                return evacuate

            section(C_Z, N_Z, gates(C_Z, ACT.Silu, lambda j: z_rows[:, :, bass.ds(j * CH, CH)], 0), peeled=1)
            section(C_GATES, N_GATES,
                    gates(C_GATES, ACT.Sigmoid, lambda j: gate_rows.rearrange("p (c b) t -> p c (b t)", b=4)
                          [:, bass.ds(j, 1), :].rearrange("p c (a n) -> p (c a) n", a=2), 8 * N_Z), peeled=1)

            def conv_turned(j):
                act.wait_ge(conv_turn, j + 1)
                for s in range(NS):
                    ins = act.activation(xs_t[:, bass.ds(j, 1), s, :].rearrange("p a n -> p (a n)"), psum[4 + s][:], ACT.Copy)
                    ins.then_inc(turn_copied, 1)

            def conv_act(j, out):
                act.wait_ge(conv_done, 4 * j + 4)
                act.activation(out, conv[:], ACT.Silu).then_inc(conv_silu, 1)

            def conv_late(j):
                if not (isinstance(j, int) and j == 0):
                    conv_turned(j - 1)
                conv_act(j, conv_s[:])

            def b_turned(j):
                act.wait_ge(conv_turn, j + 1)
                act.activation(b_t[:, 4 * (j - 8):4 * (j - 8) + 4].rearrange("p a b -> p (a b)"), psum[4][:],
                               ACT.Copy).then_inc(turn_copied, 1)

            act.wait_ge(kv_out, 32)
            nothing = lambda j, par: act.sem_inc(evac_a, 1)
            section(C_XBC, 8, nothing, peeled=1, late=conv_late)
            lates = {8: lambda: conv_late(7),
                     9: lambda: (conv_turned(7), conv_act(8, b_f[:, 0:4])),
                     10: lambda: (b_turned(8), conv_act(9, b_f[:, 4:8])),
                     11: lambda: (b_turned(9), conv_act(10, c_f[:, 0:4]))}
            for j in range(8, N_XBC):
                unit(C_XBC + j, lambda: nothing(j, 0), lates[j])

            act_dt = lambda: act.sem_inc(evac_a, 1)
            unit(C_DT, act_dt, lambda: conv_act(11, c_f[:, 4:8]))
            act.wait_ge(cache_in, 16 * 11)
            act.activation(dt_par[:, 2:4], dt_par[:, 2:4], ACT.Exp).then_inc(dt_exp, 1)
            act.wait_ge(dt_ready, 1)
            act.activation(da_t[:], da_t[:], ACT.Exp, scale=-1.0).then_inc(dt_exp, 1)
            act.wait_ge(dt_ready, 2)
            act.activation(dt_l[:], dt_w[:], ACT.Ln).then_inc(dt_exp, 1)

            act.wait_ge(ssd_acs, 1)
            act.activation(e_acs[:].rearrange("p a h -> p (a h)"), psum[4][:, 0:4 * SSD_HEADS], ACT.Exp) \
                .then_inc(ssd_e, 1)

            def decays(g, s, first=False):
                act.wait_ge(ssd_seg, 2 * g + s + 1)
                if not first:
                    act.wait_ge(ssd_mix, 2 * g + s - 1)
                for n in range(2):
                    ins = act.activation(decay_s[:, s, 4 * n:4 * n + 4].rearrange("p a b -> p (a b)"),
                                         psum[2 * s + n][:], ACT.Exp)
                ins.then_inc(ssd_exp, 1)

            def norm(g, s, first=False):
                u = 2 * g + s
                act.wait_ge(ssd_yw, u + 1)
                if not first:
                    act.wait_ge(ssd_yt, u - 1)
                act.activation(y_n[:, s], y_w[:, s], ACT.Square, accum_out=small[:, 8 + s:9 + s]).then_inc(ssd_rms, 1)
                act.wait_ge(ssd_rms, 3 * u + 1)
                act.activation(small[:, 10 + s:11 + s], small[:, 8 + s:9 + s], ACT.Ln, bias=EPS, scale=1.0 / CH) \
                    .then_inc(ssd_rms, 1)
                act.wait_ge(ssd_rms, 3 * u + 2)
                act.activation(small[:, 10 + s:11 + s], small[:, 10 + s:11 + s], ACT.Exp, scale=-0.5) \
                    .then_inc(ssd_rms, 1)
                act.wait_ge(ssd_rms, 3 * u + 3)
                act.activation(y_n[:, s], y_w[:, s], ACT.Copy, scale=small[:, 10 + s:11 + s]).then_inc(ssd_yn, 1)

            def result(g, s):
                act.wait_ge(ssd_yt, 2 * g + s + 1)
                for b in range(4):
                    ins = act.activation(y_f[:, bass.ds(4 * g + b, 1), s * P:(s + 1) * P].rearrange("p a t -> p (a t)"),
                                         psum[4][:, b * P:(b + 1) * P], ACT.Copy,
                                         scale=par_f[:, 1, bass.ds(96 + 4 * g + b, 1)])
                ins.then_inc(ssd_ytc, 1)

            def initial(g, first=False):
                act.wait_ge(ssd_s0, g + 1)
                if not first:
                    act.wait_ge(ssd_aux, 2 * g)
                for d in range(2):
                    ins = act.activation(s0_t[:, d], psum[6 + d][:], ACT.Copy)
                ins.then_inc(ssd_s0c, 1)

            final = [o[f"new_ssd_{d}"][0, 0].rearrange("h p n -> (h p) n").rearrange("(g b r) n -> r g b n", b=4, r=P)
                     for d in ("fwd", "bwd")]

            def states(g, first=False):
                act.wait_ge(ssd_aux, 2 * g + 1)
                if not first:
                    act.wait_ge(st_saved, 32 * g)
                for d in range(2):
                    ins = act.activation(st_out[:, d].rearrange("p a b -> p (a b)"), psum[6 + d][:], ACT.Copy)
                ins.then_inc(ssd_stc, 1)
                act.wait_ge(ssd_stc, g + 1)
                for d in range(2):
                    act.dma_start(final[d][:, bass.ds(g, 1)].rearrange("r g b n -> r (g b) n"), st_out[:, d]) \
                        .then_inc(st_saved, 16)

            def group(g, first=False):
                decays(g, 0, first)
                if not first:
                    norm(g - 1, 1, first=isinstance(g, int) and g == 1)
                    result(g - 1, 0)
                decays(g, 1, first)
                initial(g, first)
                states(g, first)
                norm(g, 0, first)
                if not first:
                    result(g - 1, 1)
            group(0, first=True)
            group(1)
            with act.Fori(2, GROUPS) as g:
                group(g)
            norm(GROUPS - 1, 1)
            result(GROUPS - 1, 0)
            result(GROUPS - 1, 1)

            act.wait_ge(ssd_ytc, 2 * GROUPS)
            for q in range(4):
                act.activation(na_hi[:, 4 * q:4 * q + 4], na_f[:, 4 * q:4 * q + 4], ACT.Copy).then_inc(na_split, 1)
            act.wait_ge(na_ready, 4)

            def y_part(half):
                for q in range(4):
                    b = KT * half + 4 * q
                    act.activation(y_hi[:, b:b + 4], y_f[:, b:b + 4], ACT.Copy).then_inc(y_split, 1)
            y_part(1)

            section(C_NAP, N_NAP, nothing)

            def mix_parts(j):
                act.sem_inc(evac_a, 1)
                act.wait_ge(mix_sum, j + 1)
                act.activation(mix_hi[:, bass.ds(4 * j, 4)], mix_f[:, bass.ds(4 * j, 4)], ACT.Copy).then_inc(mix_split, 1)

            def ssd_pair(i, first=False):
                for p in range(2):
                    j = 2 * i + p
                    unit(C_SSDP + 2 * j, lambda: nothing(0, 0), (lambda: y_part(0)) if first and p == 0 else None,
                         late_at=4)
                    unit(C_SSDP + 2 * j + 1, lambda: mix_parts(j))
            ssd_pair(0, first=True)
            with act.Fori(1, N_SSDP // 4) as i:
                ssd_pair(i)

            def g1_copy(j, par):
                p = (par + C_OUT) % 2
                act.wait_ge(g1_bc, j + 1)
                act.wait_ge(evac_v, C_OUT + j - 1)
                for s in range(NS):
                    ins = act.activation(g1_b[:, p, s], psum[4 + s][:], ACT.Copy)
                ins.then_inc(evac_a, 1)
            section(C_OUT, N_OUT, g1_copy)

            act.wait_ge(x2_ready, N_OUT)
            for s in range(NS):
                act.activation(xn2_t[:, s, :], x2_t[:, s, :], ACT.Square, accum_out=small[:, 16 + s:17 + s]) \
                    .then_inc(sumsq, 1)
            act.wait_ge(sumsq, 2 * NS)
            act.activation(small[:, 18:20], small[:, 16:18], ACT.Sqrt, bias=EPS, scale=1.0 / D).then_inc(rms_done, 1)

            def h2_copy(q):
                act.wait_ge(h2_turn, q + 1)
                for s in range(NS):
                    ins = act.activation(h2_t[:, s, q * CH:(q + 1) * CH], psum[2 * (q % 2) + s][:], ACT.Copy)
                ins.then_inc(h2_copied, 1)
            for q in range(4):
                act.wait_ge(nt_mod, 8 * (4 + q) + 8)
                act.activation(h_hi[:, 4 * q:4 * q + 4, :], mod_tmp[:], ACT.Copy).then_inc(nt_hi, 1)
                h2_copy(q)
            act.wait_ge(keys_turn, 1)
            act.wait_ge(nt_lo, 8)
            for n in range(4):
                ins = act.activation(keys_t[:, 4 * n:4 * n + 4].rearrange("p a b -> p (a b)"), psum[4 + n][:], ACT.Copy)
            ins.then_inc(keys_ready, 1)

            def queries(j):
                act.activation(peer_q[:, 4 * j:4 * j + 2, :], acc[(C_WQ + j) % 2][0][:].rearrange("p (b t) -> p b t", b=2),
                               ACT.Copy).then_inc(evac_a, 1)
            for j in range(N_WQ):
                unit(C_WQ + j, lambda: queries(j), last=j == N_WQ - 1)

            for s in range(NS):
                act.wait_ge(score_done, s + 1)
                for n in range(4):
                    ins = act.activation(score[:, s, 4 * n:4 * n + 4].rearrange("p a b -> p (a b)"),
                                         psum[4 - 4 * s + n][:], ACT.Copy)
                ins.then_inc(score_in, 1)
            for s in range(NS):
                act.wait_ge(gate_max, s + 1)
                act.activation(gate_t[:, s], gate_t[:, s], ACT.Exp).then_inc(gate_exp, 1)

            for s in range(NS):
                with act.Fori(0, SEL // UNROLL) as i:
                    for n in range(UNROLL):
                        e, r = s * SEL + UNROLL * i + n, n % RING
                        act.wait_ge(u_used, e + 1)
                        act.activation(gelu_c[:, r:r + 1], act_c[:, r:r + 1], ACT.Gelu).then_inc(gelu_done, 1)
                        act.wait_ge(gelu_done, e + 1)
                        act.wait_ge(staged, 2 * e + 2)
                        act.activation(coef_c[:, r:r + 1], gelu_c[:, r:r + 1], ACT.Copy, scale=gate_c[:, r:r + 1]) \
                            .then_inc(coef_ready, 1)
                act.wait_ge(x3_ready, s + 1)
                act.activation(peer_t[:, s], x2_t[:, s], ACT.Square, accum_out=small[:, 20 + s:21 + s]).then_inc(x3_rms, 1)
                act.wait_ge(x3_rms, 2 * s + 1)
                act.activation(small[:, 22 + s:23 + s], small[:, 20 + s:21 + s], ACT.Sqrt, bias=EPS, scale=1.0 / D) \
                    .then_inc(x3_rms, 1)

        @block.vector
        def _(dve):
            mark, link, enter, leave = steps_of(dve, dve_chain)

            def split(c, h, first=False):
                dve.wait_ge(hi_done, c * HALVES + h + 1)
                if not first:
                    dve.wait_ge(split_used, c * HALVES + h - 1)
                dve.tensor_tensor(w_lo[:, h % 2], raw[:, h // 2, 2 * (h % 2):2 * (h % 2) + 2, :],
                                  w_hi[:, h % 4].bitcast(F32), ALU.subtract).then_inc(lo_done, 1)

            def unit(c, evacuate, late=None, late_at=4, last=False):
                for h in range(2, HALVES):
                    split(c, h)
                    if h == late_at and late is not None:
                        late()
                if not last:
                    split(c + 1, 0)
                    split(c + 1, 1)
                dve.wait_ge(split_used, c * HALVES + HALVES)
                evacuate()

            def section(c0, n, evacuate, peeled=0, late=None, steps=0):
                for j in range(2 * peeled):
                    unit(c0 + j, lambda: evacuate(j, (c0 + j) % 2), (lambda: late(j - 1)) if late and j else None)
                with dve.Fori(peeled, n // 2) as i:
                    enter((i - peeled) * (2 * steps))
                    for p in range(2):
                        j = 2 * i + p
                        unit(c0 + j, lambda: evacuate(j, (c0 + p) % 2), (lambda: late(j - 1)) if late else None)
                    leave(n // 2 - peeled, 2 * steps)

            def nothing(j, par):
                dve.sem_inc(evac_v, 1)

            def par_copy(n):
                dve.wait_ge(par_t, n + 1)
                rows = P if n < 3 else 96
                dve.tensor_copy(par_f[:, n, 0:rows], psum[4 + n][:, 0:rows]).then_inc(par_done, 1)
            for n in range(4):
                par_copy(n)
            dve.wait_ge(c_silu, 1)
            dve.tensor_tensor(c4[:, :, 2:4], silu_c[:].rearrange("p s k -> p k s"), c4[:, :, 0:2].bitcast(F32),
                              ALU.subtract).then_inc(c_ready, 1)

            dve.wait_ge(rms_done, 1)
            link(dve.reciprocal(small[:, 2:4], small[:, 2:4]))
            for s in range(NS):
                ins = dve.tensor_scalar(x_t[:, s, :], x_t[:, s, :], small[:, 2 + s:3 + s], None, ALU.mult)
                ins.then_inc(xn_ready, 1)

            split(C_ADA, 0, first=True)
            split(C_ADA, 1, first=True)

            def ada(j, par):
                dve.wait_ge(row_used, j + 1)
                dve.tensor_copy(mod_f[:, bass.ds(4 * j, 4), :],
                                acc[par][1][:, 0:8].rearrange("p (b s) -> p b s", b=4)).then_inc(evac_v, 1)
            section(C_ADA, N_ADA, ada)

            dve.wait_ge(evac_v, N_ADA)
            dve.wait_ge(par_done, 4)
            link(dve.tensor_tensor(mod_f[:], mod_f[:], par_f[:, 0, 0:96].unsqueeze(2).broadcast_to([P, 96, NS]),
                                         ALU.add))
            for n, b in ((0, KT), (1, 4 * KT)):
                link(dve.tensor_scalar(scale_f[:, n], mod_f[:, b:b + KT, :], 1.0, None, ALU.add))
                g = par_f[:, 0, 96 + n * KT:96 + (n + 1) * KT].unsqueeze(2).broadcast_to([P, KT, NS])
                link(dve.tensor_tensor(scale_f[:, n], scale_f[:, n], g, ALU.mult))

            def modulate(norm, group0):
                for q in range(4):
                    dve.wait_ge(nt_full, group0 + q + 1)
                    if group0 + q:
                        dve.wait_ge(nt_lo, group0 + q)
                        dve.wait_ge(nt_hi, group0 + q)
                    if norm == 1 and q:
                        dve.wait_ge(h2_turn, q)
                    for k in range(4):
                        for s in range(NS):
                            b = 4 * q + k
                            ins = dve.tensor_scalar(mod_tmp[:, k, s * P:(s + 1) * P],
                                                    psum[4 + 2 * (q % 2) + k // 2][:, (k % 2) * T + s * P:(k % 2) * T + (s + 1) * P],
                                                    scale_f[:, norm, b, s:s + 1],
                                                    mod_f[:, 3 * KT * norm + b, s:s + 1], ALU.mult, ALU.add)
                            ins.then_inc(nt_mod, 1)
                    dve.wait_ge(nt_hi, group0 + q + 1)
                    dve.tensor_tensor(h_lo[:, 4 * q:4 * q + 4, :], mod_tmp[:], h_hi[:, 4 * q:4 * q + 4, :].bitcast(F32),
                                      ALU.subtract).then_inc(nt_lo, 1)
            modulate(0, 0)

            def qk(j, par):
                dve.tensor_copy(qk_f[:, bass.ds(4 * j + 2, 2), :],
                                acc[par][1][:].rearrange("p (b t) -> p b t", b=2)).then_inc(evac_v, 1)
            section(C_QK, N_QK, qk)

            def v(j, par):
                dve.tensor_copy(v_t[:, 1, bass.ds(j * CH, CH)], acc[par][1][:]).then_inc(evac_v, 1)
            section(C_V, N_V, v)

            SCALE = float(P) ** -0.5

            def maxima(h, p):
                dve.wait_ge(att_s, h + 1)
                if not isinstance(h, int):
                    dve.wait_ge(att_pt, h - 1)
                s = psum[4 + p]
                dve.tensor_scalar(soft[:, p, 0:2].rearrange("p a b -> p (a b)"), s[:, 0:2 * P], SCALE, None,
                                  ALU.mult).then_inc(att_m, 1)
                dve.scalar_tensor_tensor(out=soft[:, p, 2], in0=s[:, 2 * P:3 * P], scalar=SCALE,
                                         in1=bias_w[:, bass.ds(h, 1)].rearrange("p a b c -> p (a b c)"),
                                         op0=ALU.mult, op1=ALU.add).then_inc(att_m, 1)
                dve.wait_ge(att_m, 4 * h + 2)
                dve.tensor_reduce(stats[:, p, 0:1], soft[:, p, 0], AX.X, ALU.max, negate=True).then_inc(att_m, 1)
                dve.tensor_reduce(stats[:, p, 1:2], soft[:, p, 1:3].rearrange("p a b -> p (a b)"), AX.X, ALU.max,
                                  negate=True).then_inc(att_m, 1)

            def probabilities(h, p):
                dve.wait_ge(att_e, 2 * h + 2)
                dve.reciprocal(stats[:, p, 2:4], stats[:, p, 2:4]).then_inc(att_p, 1)
                dve.wait_ge(att_p, 3 * h + 1)
                dve.tensor_scalar(soft[:, p, 0], soft[:, p, 0], stats[:, p, 2:3], None, ALU.mult).then_inc(att_p, 1)
                dve.tensor_scalar(soft[:, p, 1:3], soft[:, p, 1:3], stats[:, p, 3:4], None, ALU.mult) \
                    .then_inc(att_p, 1)

            def head_out(h, p):
                dve.wait_ge(att_o, h + 1)
                dve.tensor_copy(na_f[:, bass.ds(h, 1), :].rearrange("p a t -> p (a t)"), psum[2 + p][:, 0:T]) \
                    .then_inc(att_oc, 1)

            dve.wait_ge(bias_turn, 1)
            for n in range(4):
                dve.tensor_tensor(bias_w[:, 4 * n:4 * n + 4], psum[4 + n][:].rearrange("p (h r k) -> p h r k", h=4, r=2),
                                  window[:].unsqueeze(1).broadcast_to([P, 4, 2, GRID_W]), ALU.add).then_inc(bias_done, 1)
            dve.wait_ge(bias_done, 4)
            maxima(0, 0)
            probabilities(0, 0)
            maxima(1, 1)
            head_out(0, 0)
            probabilities(1, 1)
            with dve.Fori(1, NA_HEADS // 2) as i:
                for p in range(2):
                    h = 2 * i + p
                    maxima(h, p)
                    head_out(h - 1, 1 - p)
                    probabilities(h, p)
            head_out(NA_HEADS - 1, 1)

            section(C_Z, N_Z, nothing)
            section(C_GATES, N_GATES, nothing)

            place = {0: (1, 0), 1: (1, 48), 2: (2, 0), 3: (2, 48), 4: (3, 0), "bias": (3, 48)}

            def convolve(j, par, bank):
                if not (isinstance(j, int) and j == 0):
                    dve.wait_ge(conv_silu, j)
                def column(tap, b):
                    n, at_ = place[tap]
                    return par_f[:, n, bass.ds(4 * j + (at_ + b), 1)]
                last = {}
                for tap in (2, 0, 1, 3, 4):
                    for b in (2 * bank, 2 * bank + 1):
                        x = acc[par][bank][:, (b % 2) * T:(b % 2 + 1) * T].rearrange("p (s t) -> p s t", s=NS)
                        y = conv[:, b].rearrange("p (s t) -> p s t", s=NS)
                        if tap == 2:
                            ins = dve.tensor_scalar(y, x, column(tap, b), column("bias", b), ALU.mult, ALU.add)
                        else:
                            dve.wait_ge(dve_chain, last[b])
                            off = tap - TAPS // 2
                            to, of = slice(max(0, -off), P - max(0, off)), slice(max(0, off), P + min(0, off))
                            ins = dve.scalar_tensor_tensor(out=y[:, :, to], in0=x[:, :, of], scalar=column(tap, b),
                                                           in1=y[:, :, to], op0=ALU.mult, op1=ALU.add)
                        if tap == TAPS - 1:
                            ins.then_inc(conv_done, 1)
                        else:
                            last[b] = mark(ins)

            def conv_first(j, par):
                convolve(j, par, 0)

            def conv_second(j, par):
                convolve(j, par, 1)
                dve.wait_ge(conv_done, 4 * j + 4)
                dve.sem_inc(evac_v, 1)

            for j in range(2):
                unit(C_XBC + j, lambda: conv_first(j, j), (lambda: conv_second(0, 0)) if j else None)
            with dve.Fori(1, 4) as i:
                enter((i - 1) * 32)
                for p in range(2):
                    j = 2 * i + p
                    unit(C_XBC + j, lambda: conv_first(j, p), lambda: conv_second(j - 1, 1 - p))
                leave(3, 32)
            for j in range(8, N_XBC):
                unit(C_XBC + j, lambda: conv_first(j, j % 2), lambda: conv_second(j - 1, 1 - j % 2))

            def dt_sum():
                dve.wait_ge(cache_in, 16 * 11)
                for s in range(NS):
                    x = acc[C_DT % 2][s][:, 0:P].rearrange("p (d h) -> p d h", d=2)
                    ins = dve.tensor_tensor(dt_t[:, s], x, dt_par[:, 0:2], ALU.add)
                ins.then_inc(evac_v, 1)
            unit(C_DT, dt_sum, lambda: conv_second(N_XBC - 1, 1))
            dve.wait_ge(evac_v, C_DT + 1)
            dve.scalar_tensor_tensor(out=da_t[:], in0=dt_t[:], scalar=-1.0, in1=dt_t[:], op0=ALU.mult,
                                     op1=ALU.max).then_inc(dt_ready, 1)
            dve.wait_ge(dt_exp, 2)
            dve.tensor_scalar(dt_w[:], da_t[:], 1.0, None, ALU.add).then_inc(dt_ready, 1)
            dve.wait_ge(dt_exp, 3)
            link(dve.tensor_scalar(dt_w[:], dt_w[:], -1.0, None, ALU.add))
            link(dve.scalar_tensor_tensor(out=dt_l[:], in0=dt_w[:], scalar=0.0, in1=dt_l[:],
                                                op0=ALU.is_equal, op1=ALU.add))
            link(dve.scalar_tensor_tensor(out=dt_w[:], in0=dt_w[:], scalar=0.0, in1=dt_w[:],
                                                op0=ALU.is_equal, op1=ALU.add))
            link(dve.reciprocal(dt_w[:], dt_w[:]))
            link(dve.tensor_tensor(dt_l[:], dt_l[:], dt_w[:], ALU.mult))
            link(dve.tensor_tensor(dt_l[:], dt_l[:], da_t[:], ALU.mult))
            link(dve.scalar_tensor_tensor(out=dt_t[:], in0=dt_t[:], scalar=0.0, in1=dt_l[:],
                                                op0=ALU.max, op1=ALU.add))
            a_b = dt_par[:, 2:4].unsqueeze(1).broadcast_to([P, NS, 2, SSD_HEADS])
            dve.scalar_tensor_tensor(out=da_t[:], in0=a_b, scalar=-1.0, in1=dt_t[:], op0=ALU.mult,
                                     op1=ALU.mult).then_inc(dt_ready, 1)

            dve.wait_ge(ssd_e, 1)
            for p in range(2):
                dve.wait_ge(gate_saved[p], 8 * (N_Z + N_GATES))

            def heads(x, g, width=HD):
                return x[:, bass.ds(g * HPG, HPG)].unsqueeze(2).broadcast_to([P, HPG, width])

            def by_head(x):
                return x.rearrange("p (h d) -> p h d", h=HPG)

            def operands(g, s, first=False):
                u = 2 * g + s
                dve.wait_ge(ssd_cb, u + 1)
                if not first:
                    dve.wait_ge(ssd_mix, u)
                for d, mask in enumerate((up_eq, low_eq)):
                    ins = dve.tensor_tensor(cbm[:, d], psum[4][:, 0:P], mask[:], ALU.mult)
                ins.then_inc(ssd_cbm, 1)
                if not first:
                    dve.wait_ge(ssd_y, u)
                x = xs_t[:, bass.ds(g, 1), s, :].rearrange("p a (h d) -> p (a h) d", h=HPG)
                for d in range(2):
                    v_ = mark(dve.tensor_tensor(by_head(xdt[:, d]), x, heads(dt_t[:, s, d], g), ALU.mult))
                dve.wait_ge(ssd_cbm, u + 1)
                dve.wait_ge(ssd_exp, u + 1)
                for d in range(2):
                    ins = dve.tensor_tensor(mix_s[:, d], decay_s[:, s],
                                            cbm[:, d].unsqueeze(1).broadcast_to([P, HPG, P]), ALU.mult)
                if s == 0:
                    if not first:
                        dve.wait_ge(ssd_aux, u - 1)
                    dve.wait_ge(dve_chain, v_)
                    for d in range(2):
                        ins = dve.tensor_tensor(by_head(xdec[:, d]), by_head(xdt[:, d]), heads(e_acs[:, 2 + d], g),
                                                ALU.mult)
                ins.then_inc(ssd_mix, 1)

            def combine(g, s, first=False):
                u = 2 * g + s
                y = y_w[:, s]
                if not first:
                    dve.wait_ge(ssd_yn, u - 1)
                x = xs_t[:, bass.ds(g, 1), s, :].rearrange("p a (h d) -> p (a h) d", h=HPG)
                link(dve.tensor_tensor(by_head(y), x, heads(dt_par[:, 4], g), ALU.mult))
                dve.wait_ge(ssd_y, u + 1)
                link(dve.tensor_tensor(y, y, psum[5][:], ALU.add))
                if s == 1:
                    dve.wait_ge(ssd_aux, u + 1)
                    for d in range(2):
                        link(dve.tensor_tensor(by_head(y_t[:]), by_head(psum[6 + d][:]), heads(e_acs[:, d], g),
                                                     ALU.mult))
                        link(dve.tensor_tensor(y, y, y_t[:], ALU.add))
                dve.wait_ge(z_in[s], 16 * g + 16)
                dve.tensor_tensor(y, y, z_g[:, s], ALU.mult).then_inc(ssd_yw, 1)

            def group(g, first=False):
                operands(g, 0, first)
                if not first:
                    combine(g - 1, 1, first=isinstance(g, int) and g == 1)
                operands(g, 1)
                combine(g, 0, first)
            group(0, first=True)
            group(1)
            with dve.Fori(2, GROUPS) as g:
                enter((g - 2) * 12)
                group(g)
                leave(GROUPS - 2, 12)
            combine(GROUPS - 1, 1)

            dve.wait_ge(ssd_ytc, 2 * GROUPS)
            dve.wait_ge(st_saved, 32 * GROUPS)
            for q in range(4):
                dve.wait_ge(na_split, q + 1)
                dve.tensor_tensor(na_lo[:, 4 * q:4 * q + 4], na_f[:, 4 * q:4 * q + 4],
                                  na_hi[:, 4 * q:4 * q + 4].bitcast(F32), ALU.subtract).then_inc(na_ready, 1)

            def y_part(half):
                for q in range(4):
                    b = KT * half + 4 * q
                    dve.wait_ge(y_split, 4 * (1 - half) + q + 1)
                    ins = dve.tensor_tensor(y_lo[:, b:b + 4], y_f[:, b:b + 4], y_hi[:, b:b + 4].bitcast(F32), ALU.subtract)
                ins.then_inc(y_ready, 1)
            y_part(1)

            def na_gated(j, par):
                p = (par + C_NAP) % 2
                dve.wait_ge(gate_in[p], 8 * (j - p) + 16)
                for b in range(2):
                    ins = dve.tensor_tensor(mix_f[:, bass.ds(4 * j + 2 * b, 2), :],
                                            acc[par][b][:].rearrange("p (b t) -> p b t", b=2),
                                            gate_g[:, p, 2 * b:2 * b + 2], ALU.mult)
                ins.then_inc(evac_v, 1)
            section(C_NAP, N_NAP, na_gated)

            def mix_parts(j, p, i):
                dve.wait_ge(gate_in[p], 16 * i + 48)
                for b in range(2):
                    ins = dve.tensor_tensor(gated[:, 2 * b:2 * b + 2], acc[(C_SSDP + p) % 2][b][:]
                                            .rearrange("p (b t) -> p b t", b=2), gate_g[:, p, 2 * b:2 * b + 2], ALU.mult)
                ins.then_inc(evac_v, 1)
                dve.wait_ge(evac_v, C_SSDP + 2 * j + 2)
                m = mix_f[:, bass.ds(4 * j, 4)]
                dve.tensor_tensor(m, m, gated[:], ALU.add).then_inc(mix_sum, 1)
                dve.wait_ge(mix_sum, j + 1)
                dve.wait_ge(mix_split, j + 1)
                dve.tensor_tensor(mix_lo[:, bass.ds(4 * j, 4)], m, mix_hi[:, bass.ds(4 * j, 4)].bitcast(F32),
                                  ALU.subtract).then_inc(mix_ready, 1)

            def ssd_pair(i, first=False):
                for p in range(2):
                    j = 2 * i + p
                    unit(C_SSDP + 2 * j, lambda: nothing(0, 0), (lambda: y_part(0)) if first and p == 0 else None)
                    unit(C_SSDP + 2 * j + 1, lambda: mix_parts(j, p, i))
            ssd_pair(0, first=True)
            with dve.Fori(1, N_SSDP // 4) as i:
                ssd_pair(i)

            dve.wait_ge(x2_in, 16 * 6)

            def residual(j, par):
                p = (par + C_OUT) % 2
                dve.wait_ge(evac_a, C_OUT + j + 1)
                for s in range(NS):
                    ins = dve.tensor_tensor(res[:, s], acc[par][s][:], g1_b[:, p, s], ALU.mult)
                ins.then_inc(evac_v, 1)
                dve.wait_ge(evac_v, C_OUT + j + 1)
                x = x2_t[:, :, bass.ds(j * CH, CH)]
                dve.tensor_tensor(x, x, res[:], ALU.add).then_inc(x2_ready, 1)
                dve.wait_ge(x2_ready, j + 1)
            section(C_OUT, N_OUT, residual)

            dve.wait_ge(rms_done, 2)
            link(dve.reciprocal(small[:, 18:20], small[:, 18:20]))
            for s in range(NS):
                dve.tensor_scalar(xn2_t[:, s, :], x2_t[:, s, :], small[:, 18 + s:19 + s], None, ALU.mult) \
                    .then_inc(xn_ready, 1)
            modulate(1, 4)

            def queries(j):
                dve.tensor_copy(peer_q[:, 4 * j + 2:4 * j + 4, :],
                                acc[(C_WQ + j) % 2][1][:].rearrange("p (b t) -> p b t", b=2)).then_inc(evac_v, 1)
            for j in range(N_WQ):
                unit(C_WQ + j, lambda: queries(j), last=j == N_WQ - 1)

            def top16(n, x, values, indices):
                for r in range(2):
                    out = slice(8 * r, 8 * r + 8)
                    for b in range(n):
                        ins = dve.max(values[:, b, out], x(b))
                    link(ins)
                    for b in range(n):
                        ins = dve.max_index(indices[:, b, out], values[:, b, out], x(b))
                    link(ins)
                    if r == 0:
                        for b in range(n):
                            ins = dve.match_replace(x(b), values[:, b, out], x(b), LOWEST)
                        link(ins)

            def select(s):
                dve.wait_ge(score_in, s + 1)
                top16(2 * PEER_HEADS, lambda b: score[:, s, b], top_v, top_i)
                dve.wait_ge(score_done, NS)
                pair = top_v[:].rearrange("p (h q) k -> p h q k", q=2)
                full = [P, PEER_HEADS, TOPK, TOPK]
                link(dve.tensor_tensor(cand[:].rearrange("p h (i j) -> p h i j", i=TOPK),
                                             pair[:, :, 0].unsqueeze(3).broadcast_to(full),
                                             pair[:, :, 1].unsqueeze(2).broadcast_to(full), ALU.add))
                top16(PEER_HEADS, lambda h: cand[:, h], cand_v, cand_i)
                gate = gate_t[:, s].rearrange("p (h k) -> p h k", h=PEER_HEADS)
                sixteen = [P, PEER_HEADS, TOPK]
                dve.tensor_tensor(gate, cand_v[:], cand_v[:, :, 0:1].broadcast_to(sixteen), ALU.subtract) \
                    .then_inc(gate_max, 1)
                flat = cand_i[:].rearrange("p h k -> p (h k)")
                dve.tensor_scalar(part_i[:, 0], flat, 4, None, ALU.logical_shift_right)
                dve.tensor_scalar(part_i[:, 1], flat, TOPK - 1, None, ALU.bitwise_and)
                link(dve.tensor_copy(top_f[:], top_i[:]))
                link(dve.tensor_copy(part_f[:], part_i[:]))
                keys = top_f[:].rearrange("p (h q) k -> p h q k", q=2)
                iota = small[:, 32:32 + TOPK].unsqueeze(1).broadcast_to([P, SEL, TOPK])
                for q in range(2):
                    link(dve.tensor_tensor(hot[:], part_f[:, q].unsqueeze(2).broadcast_to([P, SEL, TOPK]), iota,
                                                 ALU.is_equal))
                    by_place = hot[:].rearrange("p (h k) i -> p h k i", h=PEER_HEADS)
                    link(dve.tensor_tensor(by_place, by_place, keys[:, :, q].unsqueeze(2).broadcast_to(full),
                                                 ALU.mult))
                    link(dve.tensor_reduce(key_f[:, q], hot[:], AX.X, ALU.add))
                link(dve.scalar_tensor_tensor(out=key_f[:, 0], in0=key_f[:, 0], scalar=float(P), in1=key_f[:, 1],
                                                    op0=ALU.mult, op1=ALU.add))
                link(dve.tensor_copy(expert[:, s], key_f[:, 0]))
                dve.wait_ge(gate_exp, s + 1)
                link(dve.tensor_reduce(gate_sum[:], gate, AX.X, ALU.add))
                link(dve.reciprocal(gate_sum[:], gate_sum[:]))
                dve.tensor_tensor(gate, gate, gate_sum[:].unsqueeze(2).broadcast_to(sixteen), ALU.mult) \
                    .then_inc(chosen, 1)
                dve.wait_ge(chosen, s + 1)
            for s in range(NS):
                select(s)

            def expert_act(e, s, n, i):
                r = n % RING
                dve.wait_ge(u_in[r], 16 * (s * SEL // RING + UNROLL // RING * i + n // RING) + 16)
                dve.tensor_tensor_reduce(out=u_r[:, r], in0=u_r[:, r], in1=h2_t[:, s], scale=1.0, scalar=0.0,
                                         op0=ALU.mult, op1=ALU.add, accum_out=act_c[:, r:r + 1]).then_inc(u_used, 1)

            def expert_add(e, s, n, i):
                r = n % RING
                dve.wait_ge(v_in[r], 16 * (s * SEL // RING + UNROLL // RING * i + n // RING) + 16)
                dve.wait_ge(coef_ready, e + 1)
                dve.wait_ge(v_used, e + 1 + s)
                dve.scalar_tensor_tensor(out=peer_t[:, s], in0=v_r[:, r], scalar=coef_c[:, r:r + 1], in1=peer_t[:, s],
                                         op0=ALU.mult, op1=ALU.add).then_inc(v_used, 1)

            for s in range(NS):
                dve.memset(peer_t[:, s], 0.0).then_inc(v_used, 1)
                with dve.Fori(0, SEL // UNROLL) as i:
                    for n in range(UNROLL):
                        e = s * SEL + UNROLL * i + n
                        expert_act(e, s, n, i)
                        if n:
                            expert_add(e - 1, s, n - 1, i)
                    expert_add(e, s, n, i)
                dve.wait_ge(v_used, (s + 1) * (SEL + 1))
                dve.wait_ge(g2_bc, s + 1)
                for n in range(4):
                    col = slice(n * CH, (n + 1) * CH)
                    ins = dve.tensor_tensor(peer_t[:, s, col], peer_t[:, s, col], psum[4 - 4 * s + n][:], ALU.mult)
                link(ins)
                dve.tensor_tensor(x2_t[:, s], x2_t[:, s], peer_t[:, s], ALU.add).then_inc(x3_ready, 1)
                dve.wait_ge(x3_rms, 2 * s + 2)
                link(dve.reciprocal(small[:, 22 + s:23 + s], small[:, 22 + s:23 + s]))
                dve.wait_ge(x3_ready, s + 1)
                dve.wait_ge(final_in, 16)
                dve.scalar_tensor_tensor(out=peer_t[:, s], in0=x2_t[:, s], scalar=small[:, 22 + s:23 + s],
                                         in1=final_b[:], op0=ALU.mult, op1=ALU.mult).then_inc(out_ready, 1)

        @block.tensor
        def _(pe):
            def halves(c, half_slot, first=False, after_second=None):
                if not first:
                    pe.wait_ge(evac_a, c - 1)
                    pe.wait_ge(evac_v, c - 1)
                for h in range(HALVES):
                    pe.wait_ge(lo_done, c * HALVES + h + 1)
                    for kk in range(2):
                        ins = half_slot(h, kk)
                    ins.then_inc(split_used, 1)
                    if h == 1 and after_second is not None:
                        after_second()

            def part(w, h):
                return w[:, h % 4] if w is w_hi else w[:, h % 2]

            def tokens_out(par, x_hi, x_lo, k0=0, width=CH, start=True, stop=True):
                def step(h, kk):
                    k = 2 * h + kk
                    for s in range(NS):
                        t = slice(s * P, (s + 1) * P)
                        for n, (x, w) in enumerate(((x_lo, w_hi), (x_hi, w_lo), (x_hi, w_hi))):
                            ins = pe.matmul(acc[par][s][:, 0:width], x[:, k0 + k, t], part(w, h)[:, kk, 0:width],
                                            start=start and k == 0 and n == 0, stop=stop and k == KT - 1 and n == 2)
                    return ins
                return step

            def features_out(par, x_hi, x_lo, k0=0, start=True, stop=True):
                def step(h, kk):
                    k = 2 * h + kk
                    for b in range(4):
                        col = slice(b * P, (b + 1) * P)
                        for n, (w, x) in enumerate(((w_hi, x_lo), (w_lo, x_hi), (w_hi, x_hi))):
                            ins = pe.matmul(acc[par][b // 2][:, (b % 2) * T:(b % 2 + 1) * T], part(w, h)[:, kk, col],
                                            x[:, k0 + k, :], start=start and k == 0 and n == 0 and b % 2 == 0,
                                            stop=stop and k == KT - 1 and n == 2, skip_group_check=True)
                    return ins
                return step

            def section(c0, n, out, turn=None):
                peeled = 0 if turn is None else 1
                for j in range(2 * peeled):
                    halves(c0 + j, out((c0 + j) % 2))
                    if j:
                        turn(j - 1)
                with pe.Fori(peeled, n // 2) as i:
                    for p in range(2):
                        halves(c0 + 2 * i + p, out((c0 + p) % 2))
                        if turn is not None:
                            turn(2 * i + p - 1)

            pe.wait_ge(pool_const, 10 + TOPK)
            pe.wait_ge(par_in, 16 * 12)
            for n in range(4):
                rows = P if n < 3 else 96
                pe.transpose(psum[4 + n][:, 0:rows], par_rows[0:rows, n, :], ident[0:rows, 0:rows]).then_inc(par_t, 1)

            def ada_out(par):
                def step(h, kk):
                    k = 2 * h + kk
                    for n, w in enumerate((w_lo, w_hi)):
                        ins = pe.matmul(acc[par][0][0:4, :], c4[:, k, :], part(w, h)[:, kk, :],
                                        start=k == 0 and n == 0, stop=k == KT - 1 and n == 1)
                    return ins
                return step

            def ada_turn(j, par):
                pe.wait_ge(evac_a, j + 1)
                for b in range(4):
                    ins = pe.matmul(acc[par][1][:, 2 * b:2 * b + 2], row[:, par, b * P:(b + 1) * P], comb[:],
                                    start=True, stop=True)
                ins.then_inc(row_used, 1)

            pe.wait_ge(c_ready, 1)
            pe.wait_ge(pool_const, POOL_CONST)
            halves(0, ada_out(0), first=True)
            halves(1, ada_out(1), first=True, after_second=lambda: ada_turn(0, 0))
            with pe.Fori(1, N_ADA // 2) as i:
                for p in range(2):
                    j = 2 * i + p
                    halves(j, ada_out(p), after_second=lambda: ada_turn(j - 1, 1 - p))
            ada_turn(N_ADA - 1, 1)

            def norm_turn(group0, x, after=None):
                for q in range(4):
                    if group0 + q >= 2:
                        pe.wait_ge(nt_mod, 8 * (group0 + q) - 8)
                    for k in range(4):
                        for s in range(NS):
                            ins = pe.transpose(psum[4 + 2 * (q % 2) + k // 2][:, (k % 2) * T + s * P:(k % 2) * T + (s + 1) * P],
                                               x[:, s, (4 * q + k) * P:(4 * q + k + 1) * P], ident[:])
                    ins.then_inc(nt_full, 1)
                    if after is not None:
                        after(q)
            pe.wait_ge(xn_ready, NS)
            pe.wait_ge(par_done, 4)
            norm_turn(0, x_t)

            pe.wait_ge(nt_lo, 4)
            section(C_QK, N_QK, lambda par: features_out(par, h_hi, h_lo))
            pe.wait_ge(cache_in, 16 * 6)
            pe.wait_ge(nt_mod, 32)
            for n in range(4):
                ins = pe.matmul(psum[4 + n][:], flip[:], bias_w[:, 4 * n:4 * n + 4].rearrange("p h r k -> p (h r k)"),
                                start=True, stop=True)
            ins.then_inc(bias_turn, 1)
            section(C_V, N_V, lambda par: tokens_out(par, h_hi, h_lo))

            pe.wait_ge(evac_a, C_Z)
            pe.wait_ge(evac_v, C_Z)

            def scores(h, p):
                later = not isinstance(h, int)
                pe.wait_ge(att_stage, 6 * h + 6)
                if later:
                    pe.wait_ge(att_kc, 2 * h - 2)
                pe.transpose(psum[p][:, 0:P], k_s[:, p], ident[:])
                pe.transpose(psum[p][:, P:2 * P], kc_s[:, p], ident[:]).then_inc(att_kt, 1)
                if later:
                    pe.wait_ge(att_m, 4 * h - 4)
                k = qk_f[:, bass.ds(NA_HEADS + h, 1), :].rearrange("p a t -> p (a t)")
                pe.matmul(psum[4 + p][:, 0:P], q_s[:, p, 0:P], k[:, 0:P], start=True, stop=True)
                pe.matmul(psum[4 + p][:, 2 * P:3 * P], q_s[:, p, P:T], k[:, P:T], start=True, stop=True)
                pe.wait_ge(att_kc, 2 * h + 1)
                pe.matmul(psum[4 + p][:, P:2 * P], q_s[:, p, P:T], kc_f[:, p], start=True, stop=True) \
                    .then_inc(att_s, 1)

            def head(h, p, first=False):
                pe.wait_ge(att_p, 3 * h + 3)
                if not first:
                    pe.wait_ge(att_pc, h - 1)
                for n in range(3):
                    ins = pe.transpose(psum[6 + p][:, n * P:(n + 1) * P], soft[:, p, n], ident[:])
                ins.then_inc(att_pt, 1)
                pe.wait_ge(att_pc, h + 1)
                if not first:
                    pe.wait_ge(att_oc, h - 1)
                pe.matmul(psum[2 + p][:, 0:P], v_s[:, p, 0], soft_t[:, p, 0], start=True, stop=True)
                pe.matmul(psum[2 + p][:, P:T], v_s[:, p, 2], soft_t[:, p, 1], start=True, stop=False)
                pe.matmul(psum[2 + p][:, P:T], v_s[:, p, 1], soft_t[:, p, 2], start=False, stop=True) \
                    .then_inc(att_o, 1)

            pe.wait_ge(bias_done, 4)
            scores(0, 0)
            scores(1, 1)
            head(0, 0, first=True)
            with pe.Fori(1, NA_HEADS // 2) as i:
                for p in range(2):
                    h = 2 * i + p
                    scores(h, p)
                    head(h - 1, 1 - p)
            head(NA_HEADS - 1, 1)

            pe.wait_ge(att_kc, 2 * NA_HEADS)
            pe.wait_ge(att_oc, NA_HEADS)
            section(C_Z, N_Z, lambda par: tokens_out(par, h_hi, h_lo))
            section(C_GATES, N_GATES, lambda par: features_out(par, h_hi, h_lo))

            def conv_transpose(j, src, streams):
                pe.wait_ge(conv_silu, j + 1)
                if not (isinstance(j, int) and j == 0):
                    pe.wait_ge(turn_copied, 2 * j if not isinstance(j, int) or j <= 8 else 17)
                for s in range(streams):
                    for b in range(4):
                        ins = pe.transpose(psum[4 + s][:, b * P:(b + 1) * P], src[:, b, s * P:(s + 1) * P], ident[:])
                ins.then_inc(conv_turn, 1)

            out = lambda par: features_out(par, h_hi, h_lo)
            section(C_XBC, 8, out, turn=lambda j: conv_transpose(j, conv_s, NS))
            for j in range(8, N_XBC):
                halves(C_XBC + j, out(j % 2))
                if j < 11:
                    conv_transpose(j - 1, *((conv_s, NS) if j == 8 else (b_f[:, 4 * (j - 9):4 * (j - 8)], 1)))
            halves(C_DT, tokens_out(C_DT % 2, h_hi, h_lo, width=P))

            pe.wait_ge(dt_ready, 3)
            pe.wait_ge(turn_copied, 18)
            for n, (s, d, mask) in enumerate(((1, 0, up_eq), (1, 1, low_eq), (0, 0, low_st), (0, 1, up_st))):
                ins = pe.matmul(psum[4][:, n * SSD_HEADS:(n + 1) * SSD_HEADS], mask[:], da_t[:, s, d], start=True,
                                stop=True)
            ins.then_inc(ssd_acs, 1)
            pe.wait_ge(evac_v, C_DT + 1)

            def segments(g, s, first=False):
                u = 2 * g + s
                pe.wait_ge(ssd_stage, 7 * g + 4 + 2 * s)
                if first:
                    pe.wait_ge(ssd_e, 1)
                if not first:
                    if not (isinstance(u, int) and u == 2):
                        pe.wait_ge(ssd_ytc, u - 2)
                    pe.wait_ge(ssd_exp, u - 1)
                if s == 1 or not first:
                    pe.wait_ge(ssd_cbm, u)
                pe.matmul(psum[4][:, 0:P], bc_s[:, 0, s * P:(s + 1) * P], bc_s[:, 1, s * P:(s + 1) * P], start=True,
                          stop=True).then_inc(ssd_cb, 1)
                for h in range(HPG):
                    sums = psum[2 * s + h // 4][:, (h % 4) * P:(h % 4 + 1) * P]
                    pe.matmul(sums, m_s[:, s, 0, h], up_eq[:], start=True, stop=False)
                    ins = pe.matmul(sums, m_s[:, s, 1, h], low_eq[:], start=False, stop=True)
                ins.then_inc(ssd_seg, 1)

            def products(g, s, first=False):
                u = 2 * g + s
                pe.wait_ge(ssd_mix, u + 1)
                if not first:
                    pe.wait_ge(ssd_yw, u)
                for h in range(HPG):
                    for d in range(2):
                        ins = pe.matmul(psum[5][:, h * HD:(h + 1) * HD], mix_s[:, d, h], xdt[:, d, h * HD:(h + 1) * HD],
                                        start=d == 0, stop=d == 1)
                ins.then_inc(ssd_y, 1)

            def with_states(g):
                pe.wait_ge(ssd_s0c, g + 1)
                pe.wait_ge(ssd_stc, g + 1)
                pe.wait_ge(ssd_stage, 7 * g + 7)
                for d in range(2):
                    ins = pe.matmul(psum[6 + d][:], c_y[:], s0_t[:, d], start=True, stop=True)
                ins.then_inc(ssd_aux, 1)

            def final_states(g):
                pe.wait_ge(ssd_s0c, g + 1)
                for d in range(2):
                    for b in range(4):
                        ins = pe.matmul(psum[6 + d][:, b * P:(b + 1) * P], xdec[:, d, b * P:(b + 1) * P],
                                        b_t[:, bass.ds(g, 1), :].rearrange("p a n -> p (a n)"), start=True, stop=True)
                ins.then_inc(ssd_aux, 1)

            def turn_initial(g, first=False):
                pe.wait_ge(s0_in, 32 * g + 32)
                if not first:
                    pe.wait_ge(ssd_yw, 2 * g)
                for d in range(2):
                    for b in range(4):
                        ins = pe.transpose(psum[6 + d][:, b * P:(b + 1) * P], s0_raw[:, d, b], ident[:])
                ins.then_inc(ssd_s0, 1)

            def turn_result(g, s, mask_unit):
                pe.wait_ge(ssd_yn, 2 * g + s + 1)
                pe.wait_ge(ssd_cbm, mask_unit + 1)
                if s == 1:
                    pe.wait_ge(ssd_ytc, 2 * g + 1)
                for b in range(4):
                    ins = pe.transpose(psum[4][:, b * P:(b + 1) * P], y_n[:, s, b * P:(b + 1) * P], ident[:])
                ins.then_inc(ssd_yt, 1)

            def group(g, first=False):
                segments(g, 0, first)
                if not first:
                    products(g - 1, 1)
                    with_states(g - 1)
                    turn_result(g - 1, 0, 2 * g)
                segments(g, 1, first)
                turn_initial(g, first)
                products(g, 0, first)
                final_states(g)
                if not first:
                    turn_result(g - 1, 1, 2 * g + 1)
            group(0, first=True)
            group(1)
            with pe.Fori(2, GROUPS) as g:
                group(g)
            last = GROUPS - 1
            products(last, 1)
            with_states(last)
            pe.wait_ge(ssd_ytc, 2 * last)
            turn_result(last, 0, 2 * last + 1)
            turn_result(last, 1, 2 * last + 1)

            pe.wait_ge(ssd_exp, 2 * GROUPS)
            pe.wait_ge(na_ready, 4)
            section(C_NAP, N_NAP, lambda par: features_out(par, na_hi, na_lo))

            def ssd_pair(i, first=False):
                for p in range(2):
                    c, par = C_SSDP + 4 * i + 2 * p, (C_SSDP + p) % 2
                    halves(c, features_out(par, y_hi, y_lo, k0=KT, stop=False))
                    if first and p == 0:
                        pe.wait_ge(y_ready, 2)
                    halves(c + 1, features_out(par, y_hi, y_lo, start=False))
            pe.wait_ge(y_ready, 1)
            ssd_pair(0, first=True)
            with pe.Fori(1, N_SSDP // 4) as i:
                ssd_pair(i)

            def spread(bank, s, n, col):
                return pe.matmul(bank[:], comb_b[:, s], g_rows[:, n, col], start=True, stop=True)

            def spread_g1(c, j):
                pe.wait_ge(evac_a, c)
                for s in range(NS):
                    ins = spread(psum[4 + s], s, 0, bass.ds(j * CH, CH) if not isinstance(j, int)
                                 else slice(j * CH, (j + 1) * CH))
                ins.then_inc(g1_bc, 1)
            pe.wait_ge(mix_ready, 4)
            pe.wait_ge(x2_in, 16 * 6)
            pe.wait_ge(ssd_ytc, 2 * GROUPS)
            with pe.Fori(0, N_OUT // 2) as i:
                for p in range(2):
                    c = C_OUT + 2 * i + p
                    halves(c, tokens_out((C_OUT + p) % 2, mix_hi, mix_lo), after_second=lambda: spread_g1(c, 2 * i + p))

            pe.wait_ge(xn_ready, 2 * NS)
            pe.wait_ge(evac_a, C_WQ)

            def h2_back(q):
                pe.wait_ge(nt_mod, 8 * (4 + q) + 8)
                if q >= 2:
                    pe.wait_ge(h2_copied, q - 1)
                for s in range(NS):
                    for k in range(4):
                        ins = pe.transpose(psum[2 * (q % 2) + s][:, k * P:(k + 1) * P], mod_tmp[:, k, s * P:(s + 1) * P],
                                           ident[:])
                ins.then_inc(h2_turn, 1)
            norm_turn(4, xn2_t, after=h2_back)

            pe.wait_ge(keys_in, 16)
            pe.wait_ge(nt_mod, 64)
            for n in range(16):
                ins = pe.transpose(psum[4 + n // 4][:, (n % 4) * P:(n % 4 + 1) * P], keys_r[:, n], ident[:])
            ins.then_inc(keys_turn, 1)
            pe.wait_ge(nt_lo, 8)
            pe.wait_ge(h2_copied, 4)
            section(C_WQ, N_WQ, lambda par: features_out(par, h_hi, h_lo))
            pe.wait_ge(evac_a, C_END)
            pe.wait_ge(evac_v, C_END)
            pe.wait_ge(keys_ready, 1)
            for s in range(NS):
                for b in range(2 * PEER_HEADS):
                    ins = pe.matmul(psum[4 - 4 * s + b // 4][:, (b % 4) * P:(b % 4 + 1) * P],
                                    peer_q[:, b, s * P:(s + 1) * P], keys_t[:, b], start=True, stop=True)
                ins.then_inc(score_done, 1)
            for s in range(NS):
                pe.wait_ge(score_in, s + 1)
                for n in range(4):
                    ins = spread(psum[4 - 4 * s + n], s, 1, slice(n * CH, (n + 1) * CH))
                ins.then_inc(g2_bc, 1)


OUTPUTS = [("y_prompt", (1, P, D)), ("y_sample", (1, P, D)),
           ("new_na_k", (1, 1, P, NA_HEADS, P)), ("new_na_v", (1, 1, P, NA_HEADS, P)),
           ("new_ssd_fwd", (1, 1, SSD_HEADS, HD, P)), ("new_ssd_bwd", (1, 1, SSD_HEADS, HD, P))]


def kernel(**inputs):
    import numpy as np
    import concourse.bacc as bacc
    from concourse.bass_utils import run_bass_kernel_spmd

    nc = bacc.Bacc("TRN2", target_bir_lowering=False, num_devices=1)
    arrays, ins = {}, {}
    for name, value in inputs.items():
        arrays[f"in_{name}"] = np.ascontiguousarray(value)
        ins[name] = nc.dram_tensor(f"in_{name}", arrays[f"in_{name}"].shape, F32, kind="ExternalInput").ap()
    outs = {name: nc.dram_tensor(f"out_{name}", shape, F32, kind="ExternalOutput").ap() for name, shape in OUTPUTS}
    program(nc, ins, outs)
    got = run_bass_kernel_spmd(nc, [arrays], core_ids=[0]).results[0]
    return tuple(got[f"out_{name}"] for name, _ in OUTPUTS)
```
